# Optimizing a Trainium2 kernel written in Bass

```python
import math
import jax, jax.numpy as jnp
from jax import lax
import numpy as np

D_MODEL = 2048
BATCH = 1
SEQ = 256
DEPTH = 1
DEC_BATCH = 8
DEC_SEQ = 8
PAST_LEN = 2048
PAGE_SIZE = 128

N_META = 16
MIX_WIDTH = D_MODEL
GLA_WIDTH = MIX_WIDTH // 2
GLA_HEADS = 4
GLA_DV = GLA_WIDTH // GLA_HEADS
GLA_DK = GLA_DV // 2
GLA_KEY_WIDTH = GLA_HEADS * GLA_DK
GLA_RANK = 16
GLA_GATE_NORM = 16.0
GLA_CHUNK = 64
S5_WIDTH = MIX_WIDTH - GLA_WIDTH
S5_GROUP = 16
S5_GROUPS = S5_WIDTH // S5_GROUP
S5_STATE = 64
N_GROUPS = 4
EXPERTS_PER_GROUP = 8
N_EXPERTS = N_GROUPS * EXPERTS_PER_GROUP
EXPERT_HIDDEN = D_MODEL // 4
TOP_K = 2
EXPERT_BLOCK = 128
EPS = 1e-6
IN_COLS = 2 * GLA_KEY_WIDTH + 2 * GLA_WIDTH + GLA_RANK + S5_WIDTH

kernel_name = 'hymba_gla_s5_hmoe_step'

def rmsnorm(x, g):
    xf = x.astype(jnp.float32)
    y = xf * lax.rsqrt(jnp.mean(xf * xf, axis=-1, keepdims=True) + EPS) * g.astype(jnp.float32)
    return y.astype(x.dtype)

def gla_chunk(S, q, k, v, g):
    C = q.shape[1]
    b = jnp.cumsum(g, axis=1)
    o_inter = jnp.einsum('bchk,bhkv->bchv', q * jnp.exp(b), S)
    mask = jnp.tril(jnp.ones((C, C), bool))[None, :, :, None, None]
    diff = b[:, :, None] - b[:, None, :]
    decay = jnp.where(mask, jnp.exp(jnp.where(mask, diff, 0.0)), 0.0)
    scores = jnp.einsum('bihk,bjhk,bijhk->bhij', q, k, decay)
    o_intra = jnp.einsum('bhij,bjhv->bihv', scores, v)
    b_last = b[:, -1]
    k_dec = k * jnp.exp(b_last[:, None] - b)
    S_new = jnp.exp(b_last)[..., None] * S + jnp.einsum('bchk,bchv->bhkv', k_dec, v)
    return o_inter + o_intra, S_new

def gla_sequence(S0, q, k, v, g, n_lead, chunk):
    outs = []
    S = S0
    if n_lead > 0:
        o, S = gla_chunk(S, q[:, :n_lead], k[:, :n_lead], v[:, :n_lead], g[:, :n_lead])
        outs.append(o)
        q, k, v, g = q[:, n_lead:], k[:, n_lead:], v[:, n_lead:], g[:, n_lead:]
    Bsz, T = q.shape[:2]
    nc = T // chunk

    def to_chunks(t):
        return jnp.moveaxis(t.reshape((Bsz, nc, chunk) + t.shape[2:]), 1, 0)

    def step(S, inp):
        o, S = gla_chunk(S, *inp)
        return S, o

    S, o = lax.scan(step, S, (to_chunks(q), to_chunks(k), to_chunks(v), to_chunks(g)))
    outs.append(jnp.moveaxis(o, 0, 1).reshape(Bsz, T, GLA_HEADS, GLA_DV))
    return jnp.concatenate(outs, axis=1), S

def _complex_affine_combine(e1, e2):
    a1r, a1i, b1r, b1i = e1
    a2r, a2i, b2r, b2i = e2
    ar = a2r * a1r - a2i * a1i
    ai = a2r * a1i + a2i * a1r
    br = a2r * b1r - a2i * b1i + b2r
    bi = a2r * b1i + a2i * b1r + b2i
    return (ar, ai, br, bi)

def s5_mix(u, h0_re, h0_im, lam_re, lam_im, log_dt, b_re, b_im, c_re, c_im, d_skip):
    f32 = jnp.float32
    Bsz, T = u.shape[:2]
    u = u.astype(f32).reshape(Bsz, T, S5_GROUPS, S5_GROUP)
    dt = jnp.exp(log_dt.astype(f32))[:, None]
    lr, li = lam_re.astype(f32), lam_im.astype(f32)
    mag = jnp.exp(lr * dt)
    ab_re, ab_im = mag * jnp.cos(li * dt), mag * jnp.sin(li * dt)
    den = lr * lr + li * li
    f_re = ((ab_re - 1.0) * lr + ab_im * li) / den
    f_im = (ab_im * lr - (ab_re - 1.0) * li) / den
    br, bi = b_re.astype(f32), b_im.astype(f32)
    bb_re = f_re[..., None] * br - f_im[..., None] * bi
    bb_im = f_re[..., None] * bi + f_im[..., None] * br
    bu_re = jnp.einsum('gpc,btgc->btgp', bb_re, u)
    bu_im = jnp.einsum('gpc,btgc->btgp', bb_im, u)
    h0r, h0i = h0_re.astype(f32), h0_im.astype(f32)
    bu_re = bu_re.at[:, 0].add(ab_re * h0r - ab_im * h0i)
    bu_im = bu_im.at[:, 0].add(ab_re * h0i + ab_im * h0r)
    a_re = jnp.broadcast_to(ab_re, bu_re.shape)
    a_im = jnp.broadcast_to(ab_im, bu_im.shape)
    _, _, hr, hi = lax.associative_scan(_complex_affine_combine, (a_re, a_im, bu_re, bu_im), axis=1)
    y = (jnp.einsum('gcp,btgp->btgc', c_re.astype(f32), hr)
         - jnp.einsum('gcp,btgp->btgc', c_im.astype(f32), hi)
         + d_skip.astype(f32) * u)
    return y.reshape(Bsz, T, S5_WIDTH), hr[:, -1], hi[:, -1]

def hier_moe(xt, w_rg, b_rg, w_re, b_re, w_gate, w_up, w_down):
    f32 = jnp.float32
    T = xt.shape[0]
    xf = xt.astype(f32)
    lg = xf @ w_rg.astype(f32) + b_rg.astype(f32)
    pg = jax.nn.softmax(lg, axis=-1)
    gsel = jnp.argmax(lg, axis=-1)
    pg_sel = jnp.take_along_axis(pg, gsel[:, None], axis=-1)[:, 0]
    le = jnp.einsum('td,gde->tge', xf, w_re.astype(f32)) + b_re.astype(f32)
    le_sel = jnp.take_along_axis(le, gsel[:, None, None], axis=1)[:, 0]
    vals, idx = lax.top_k(le_sel, TOP_K)
    pe = jax.nn.softmax(vals, axis=-1)
    eid = (gsel[:, None] * EXPERTS_PER_GROUP + idx).reshape(-1).astype(jnp.int32)
    wts = (pg_sel[:, None] * pe).reshape(-1)
    tok = jnp.repeat(jnp.arange(T, dtype=jnp.int32), TOP_K)
    A = T * TOP_K
    order = jnp.argsort(eid)
    eid_s, tok_s, w_s = eid[order], tok[order], wts[order]
    counts = jax.ops.segment_sum(jnp.ones((A,), jnp.int32), eid, num_segments=N_EXPERTS)
    starts = jnp.cumsum(counts) - counts
    padded = (counts + EXPERT_BLOCK - 1) // EXPERT_BLOCK * EXPERT_BLOCK
    pends = jnp.cumsum(padded)
    pstarts = pends - padded
    dest = pstarts[eid_s] + jnp.arange(A, dtype=jnp.int32) - starts[eid_s]
    nb = -(-A // EXPERT_BLOCK) + N_EXPERTS
    slot_tok = jnp.full((nb * EXPERT_BLOCK,), T, jnp.int32).at[dest].set(tok_s)
    slot_w = jnp.zeros((nb * EXPERT_BLOCK,), f32).at[dest].set(w_s)
    block_exp = jnp.minimum(jnp.searchsorted(pends, jnp.arange(nb, dtype=jnp.int32) * EXPERT_BLOCK, side='right'),
                            N_EXPERTS - 1)
    xpad = jnp.concatenate([xt, jnp.zeros((1, xt.shape[1]), xt.dtype)], axis=0)

    def run_block(args):
        idx_b, e = args
        xb = xpad[idx_b]
        hb = jax.nn.silu(xb @ w_gate[e]) * (xb @ w_up[e])
        return hb @ w_down[e]

    out = lax.map(run_block, (slot_tok.reshape(nb, EXPERT_BLOCK), block_exp))
    y = jnp.zeros((T + 1, xt.shape[1]), f32).at[slot_tok].add(
        out.reshape(-1, xt.shape[1]).astype(f32) * slot_w[:, None])
    return y[:T].astype(xt.dtype)

def layer(h, S_gla, s_re, s_im, n_lead, chunk, p):
    f32 = jnp.float32
    Bsz, T, _ = h.shape
    xn = rmsnorm(h, p['g_mix'])
    proj = xn @ p['w_in']
    sizes = [GLA_KEY_WIDTH, GLA_KEY_WIDTH, GLA_WIDTH, GLA_WIDTH, GLA_RANK, S5_WIDTH]
    q, k, v, r, a_low, u = jnp.split(proj, np.cumsum(sizes)[:-1].tolist(), axis=-1)
    q = q.astype(f32).reshape(Bsz, T, GLA_HEADS, GLA_DK) * (GLA_DK ** -0.5)
    k = k.astype(f32).reshape(Bsz, T, GLA_HEADS, GLA_DK)
    v = v.astype(f32).reshape(Bsz, T, GLA_HEADS, GLA_DV)
    gk = jax.nn.log_sigmoid((a_low @ p['w_gk2'] + p['b_gk']).astype(f32)) / GLA_GATE_NORM
    gk = gk.reshape(Bsz, T, GLA_HEADS, GLA_DK)
    o, S_new = gla_sequence(S_gla.astype(f32), q, k, v, gk, n_lead, chunk)
    o = o * lax.rsqrt(jnp.mean(o * o, axis=-1, keepdims=True) + EPS) * p['g_gla'].astype(f32)
    o_gla = o.reshape(Bsz, T, GLA_WIDTH) * jax.nn.silu(r.astype(f32))
    y5, hr, hi = s5_mix(u, s_re, s_im, p['lam_re'], p['lam_im'], p['log_dt'], p['s5_b_re'], p['s5_b_im'],
                        p['s5_c_re'], p['s5_c_im'], p['d_skip'])
    z = jax.nn.gelu(y5)
    o_s5 = z * jax.nn.sigmoid(z @ p['w_glu'].astype(f32) + p['b_glu'].astype(f32))
    mixed = jnp.concatenate([o_gla, o_s5], axis=-1).astype(h.dtype)
    h = h + mixed @ p['w_out']
    hn = rmsnorm(h, p['g_ffn'])
    h = h + hier_moe(hn.reshape(-1, D_MODEL), p['w_rg'], p['b_rg'], p['w_re'], p['b_re'],
                     p['w_gate'], p['w_up'], p['w_down']).reshape(h.shape)
    return h, S_new, hr, hi

def setup_inputs(seed: int = 0) -> dict:
    key = jax.random.key(seed)
    ks = jax.random.split(key, 40)
    f32 = jnp.float32
    nrm = lambda i, shape, s: jax.random.normal(ks[i], shape, f32) * s
    L, D, G, P = DEPTH, D_MODEL, S5_GROUPS, S5_STATE
    lam_im_base = math.pi * jnp.arange(P, dtype=f32)
    return {
        'x_prompt': nrm(0, (BATCH, SEQ, D), 1.0),
        'x_sample': nrm(1, (DEC_BATCH, DEC_SEQ, D), 1.0),
        'state_gla': nrm(2, (L, DEC_BATCH, GLA_HEADS, GLA_DK, GLA_DV), 0.1),
        'state_s5_re': nrm(3, (L, DEC_BATCH, G, P), 0.5),
        'state_s5_im': nrm(4, (L, DEC_BATCH, G, P), 0.5),
        'meta': nrm(5, (N_META, D), 1.0),
        'g_mix': 1.0 + nrm(6, (L, D), 0.01),
        'w_in': nrm(7, (L, D, IN_COLS), D ** -0.5),
        'w_gk2': nrm(8, (L, GLA_RANK, GLA_KEY_WIDTH), GLA_RANK ** -0.5),
        'b_gk': nrm(9, (L, GLA_KEY_WIDTH), 0.1),
        'g_gla': 1.0 + nrm(10, (L, GLA_HEADS, GLA_DV), 0.01),
        'lam_re': -0.5 + nrm(11, (L, G, P), 0.01),
        'lam_im': lam_im_base + nrm(12, (L, G, P), 0.01),
        'log_dt': jax.random.uniform(ks[13], (L, G), f32, math.log(1e-3), math.log(1e-1)),
        's5_b_re': nrm(14, (L, G, P, S5_GROUP), (2 * S5_GROUP) ** -0.5),
        's5_b_im': nrm(15, (L, G, P, S5_GROUP), (2 * S5_GROUP) ** -0.5),
        's5_c_re': nrm(16, (L, G, S5_GROUP, P), (2 * P) ** -0.5),
        's5_c_im': nrm(17, (L, G, S5_GROUP, P), (2 * P) ** -0.5),
        'd_skip': nrm(18, (L, G, S5_GROUP), 1.0),
        'w_glu': nrm(19, (L, S5_WIDTH, S5_WIDTH), S5_WIDTH ** -0.5),
        'b_glu': nrm(20, (L, S5_WIDTH), 0.01),
        'w_out': nrm(21, (L, MIX_WIDTH, D), MIX_WIDTH ** -0.5),
        'g_ffn': 1.0 + nrm(22, (L, D), 0.01),
        'w_rg': nrm(23, (L, D, N_GROUPS), D ** -0.5),
        'b_rg': nrm(24, (L, N_GROUPS), 0.01),
        'w_re': nrm(25, (L, N_GROUPS, D, EXPERTS_PER_GROUP), D ** -0.5),
        'b_re': nrm(26, (L, N_GROUPS, EXPERTS_PER_GROUP), 0.01),
        'w_gate': nrm(27, (L, N_EXPERTS, D, EXPERT_HIDDEN), D ** -0.5),
        'w_up': nrm(28, (L, N_EXPERTS, D, EXPERT_HIDDEN), D ** -0.5),
        'w_down': nrm(29, (L, N_EXPERTS, EXPERT_HIDDEN, D), EXPERT_HIDDEN ** -0.5),
        'g_final': 1.0 + nrm(30, (D,), 0.01),
    }

def reference(x_prompt, x_sample, state_gla, state_s5_re, state_s5_im, meta, g_mix, w_in, w_gk2, b_gk,
              g_gla, lam_re, lam_im, log_dt, s5_b_re, s5_b_im, s5_c_re, s5_c_im, d_skip, w_glu, b_glu,
              w_out, g_ffn, w_rg, b_rg, w_re, b_re, w_gate, w_up, w_down, g_final):
    f32 = jnp.float32
    h_p = jnp.concatenate([jnp.broadcast_to(meta.astype(x_prompt.dtype), (x_prompt.shape[0], N_META, D_MODEL)),
                           x_prompt], axis=1)
    h_s = x_sample
    Bp, Bs = x_prompt.shape[0], x_sample.shape[0]
    chunk_s = GLA_CHUNK if x_sample.shape[1] % GLA_CHUNK == 0 else x_sample.shape[1]
    gla_p, re_p, im_p, gla_s, re_s, im_s = [], [], [], [], [], []
    for l in range(DEPTH):
        p = {'g_mix': g_mix[l], 'w_in': w_in[l], 'w_gk2': w_gk2[l], 'b_gk': b_gk[l], 'g_gla': g_gla[l],
             'lam_re': lam_re[l], 'lam_im': lam_im[l], 'log_dt': log_dt[l], 's5_b_re': s5_b_re[l],
             's5_b_im': s5_b_im[l], 's5_c_re': s5_c_re[l], 's5_c_im': s5_c_im[l], 'd_skip': d_skip[l],
             'w_glu': w_glu[l], 'b_glu': b_glu[l], 'w_out': w_out[l], 'g_ffn': g_ffn[l], 'w_rg': w_rg[l],
             'b_rg': b_rg[l], 'w_re': w_re[l], 'b_re': b_re[l], 'w_gate': w_gate[l], 'w_up': w_up[l],
             'w_down': w_down[l]}
        h_p, Sg, sr, si = layer(h_p, jnp.zeros((Bp, GLA_HEADS, GLA_DK, GLA_DV), f32),
                                jnp.zeros((Bp, S5_GROUPS, S5_STATE), f32),
                                jnp.zeros((Bp, S5_GROUPS, S5_STATE), f32), N_META, GLA_CHUNK, p)
        gla_p.append(Sg); re_p.append(sr); im_p.append(si)
        h_s, Sg, sr, si = layer(h_s, state_gla[l], state_s5_re[l], state_s5_im[l], 0, chunk_s, p)
        gla_s.append(Sg); re_s.append(sr); im_s.append(si)
    y_prompt = rmsnorm(h_p, g_final)[:, N_META:]
    y_sample = rmsnorm(h_s, g_final)
    new_gla_prompt = jnp.stack(gla_p)
    new_s5_re_prompt = jnp.stack(re_p)
    new_s5_im_prompt = jnp.stack(im_p)
    new_gla_sample = jnp.stack(gla_s)
    new_s5_re_sample = jnp.stack(re_s)
    new_s5_im_sample = jnp.stack(im_s)
    return (y_prompt, y_sample, new_gla_prompt, new_s5_re_prompt, new_s5_im_prompt,
            new_gla_sample, new_s5_re_sample, new_s5_im_sample)


_drawn_inputs = setup_inputs


def setup_inputs(seed=0):
    import zlib

    import numpy as np

    out = dict(_drawn_inputs(seed))
    spreads = {}
    factors = {'g_mix': 3.314,
     'g_gla': 46.368,
     'lam_re': 17.347,
     'b_glu': 64.0,
     'b_rg': 28.624,
     'b_re': 38.992,
     'g_final': 30.548,
     'state_gla': 2.954,
     's5_c_re': 7.361,
     's5_c_im': 7.279,
     'g_ffn': 8.0,
     'w_rg': 3.477,
     'w_re': 3.466,
     'w_gate': 3.305,
     'w_up': 3.123,
     'w_down': 3.121}
    for name, (base, spread) in spreads.items():
        noise = np.random.default_rng([zlib.crc32(name.encode()), seed]).standard_normal(out[name].shape)
        drawn = base * np.exp(spread * noise) if base else spread * noise
        out[name] = __import__('jax').numpy.asarray(drawn.astype(out[name].dtype))
    for name, factor in factors.items():
        out[name] = (out[name] * factor).astype(out[name].dtype)
    return out
```

```python
import math
from contextlib import ExitStack

import concourse.bass as bass
from concourse import mybir

F32 = mybir.dt.float32
I32 = mybir.dt.int32
U32 = mybir.dt.uint32
ALU = mybir.AluOpType
ACT = mybir.ActivationFunctionType
AX = mybir.AxisListType

D = 2048
KT = D // 128
N_META, SEQ, NSEQ, DSEQ = 16, 256, 8, 8
NPRE = N_META + SEQ
NS = NSEQ * DSEQ
T = NPRE + NS
TO = SEQ + NS
XT_ROWS = T // 3
H, DK, DV = 4, 128, 256
RANK = 16
G, P, GC = 64, 64, 16
NJ = G * P // 128
CL = 32
NCP = (NPRE + CL - 1) // CL
PADT = NCP * CL - NPRE
NCS = NS // CL
NCH = NCP + NCS
SPC = CL // DSEQ
NG, EPG, NE, HID = 4, 8, 32, 512
CAP = 64
NA = 2 * TO
NOVF = (NA - 1) // (CAP + 1)
NBLK = NE + NOVF
EPS = 1e-6
OFF_Q, OFF_K, OFF_V, OFF_R, OFF_A, OFF_U = 0, 512, 1024, 2048, 3072, 3088
MAGIC = 1.5 * 2.0 ** 23
TWO_PI_1 = 6.28125
TWO_PI_2 = 0.0019350051879882812
TWO_PI_3 = 2.0 * math.pi - TWO_PI_1 - TWO_PI_2
BIG = 3.0e38
ARENA = 53184

TILES = ([("u", c) for c in range(8)] + [("a", 0)] + [("q", h) for h in range(4)] + [("k", h) for h in range(4)]
         + [("v", m) for m in range(8)] + [("gk", h) for h in range(4)] + [("r", m) for m in range(8)]
         + [("glu", c) for c in range(8)])
TIDX = {t: i for i, t in enumerate(TILES)}
CHUNKS = ([("u", i) for i in range(4)] + [("q", i) for i in range(2)] + [("k", i) for i in range(2)]
          + [("v", i) for i in range(4)] + [("r", i) for i in range(4)] + [("glu", i) for i in range(4)]
          + [("out", i) for i in range(8)])
CIDX = {c: i for i, c in enumerate(CHUNKS)}
COL0 = {"u": OFF_U, "q": OFF_Q, "k": OFF_K, "v": OFF_V, "r": OFF_R}
GLA_TILE0 = TIDX[("r", 2)]


def s5_half_steps():
    return [5 + (j * 5) // 4 for j in range(NJ)]


class Steps:

    def __init__(self, eng, sem):
        self.eng, self.sem, self.n = eng, sem, 0

    def __call__(self, ins):
        ins.then_inc(self.sem, 1)
        self.n += 1

    def sync(self):
        if self.n:
            self.eng.wait_ge(self.sem, self.n)


class Region:
    def __init__(self, arena, start, size):
        self.arena, self.at, self.end = arena, start, start + size

    def take(self, *shape, parts=128):
        n = int(math.prod(shape))
        a = self.arena[0:parts, self.at:self.at + n]
        self.at += n
        assert self.at <= self.end, (self.at, self.end)
        if len(shape) == 1:
            return a
        names = "abcd"[:len(shape)]
        return a.rearrange(f"p ({' '.join(names)}) -> p {' '.join(names)}", **dict(zip(names[1:], shape[1:])))


def bc(ap, axis, n):
    shape = list(ap.shape)
    assert shape[axis] == 1
    shape[axis] = n
    return ap.broadcast_to(shape)


def build(nc, A):
    ctx = ExitStack()
    with ctx:
        def sem(name):
            return ctx.enter_context(nc.semaphore(name))

        arena = ctx.enter_context(nc.sbuf_tensor("arena", [128, ARENA], F32))
        ps = ctx.enter_context(nc.psum_tensor("ps", [128, 8, 512], F32))
        xg = nc.dram_tensor("xg", (NBLK * CAP, D), F32, kind="Internal").ap()
        yg = nc.dram_tensor("yg", (NBLK * CAP, D), F32, kind="Internal").ap()

        SIZE_A, SIZE_B, SIZE_C, SIZE_D = 24576, 8192, 5120, 12288
        at_b = SIZE_A
        at_c = at_b + SIZE_B
        at_d = at_c + SIZE_C
        at_x = at_d + SIZE_D
        ra = Region(arena, 0, SIZE_A)
        E = ra.take(2, 2, 4 * T)
        E = [E[:, b].rearrange("p r (j t) -> p r j t", j=4) for b in range(2)]
        at_xn = ra.at
        xnT = ra.take(KT, T)
        at_u = ra.at
        uT = ra.take(8, T)
        qT = ra.take(NCH, H, CL)
        kT = ra.take(NCH, H, CL)
        at_v = ra.at
        vT = ra.take(2, NCH, H * CL)
        rT = ra.take(8, TO)
        aT = ra.take(T, parts=RANK)
        at_g = ra.at
        bG = ra.take(NCH, H, CL)
        wgk = ra.take(H * DK, parts=RANK)
        wa = ra.take(KT, RANK)
        gmask32 = ra.take(384)
        glu_t = [Region(arena, ra.at - 384, 384).take(TO), Region(arena, at_g - T, T).take(TO)]
        xr = arena[0:XT_ROWS, at_v:at_v + 3 * D].rearrange("p (t d) -> p t d", t=3)
        r = Region(arena, at_g, NCH * H * CL)
        h0 = r.take(2, NSEQ, NJ)
        ah0 = r.take(2, NJ, NSEQ)
        r = Region(arena, 0, at_xn)
        sstate = [r.take(SPC, H, DV), Region(arena, at_xn, 4096).take(SPC, H, DV)]
        qexp = r.take(H, SPC, CL)
        junk = r.take(DV)
        PTm = [r.take(128) for _ in range(2)]
        gss = r.take(32)
        glast = r.take(68)
        o_all = Region(arena, at_u, 2688).take(NCH - 1, DV)
        r = Region(arena, 0, SIZE_A)
        wpiece = [r.take(2048) for _ in range(12)]
        yrows = [arena[:, 2048 * i:2048 * (i + 1)] for i in range(6)]
        ring = [arena[:, at_b + 4096 * i:at_b + 4096 * (i + 1)] for i in range(2)]
        r = Region(arena, at_b, SIZE_B)
        xrow = r.take(D, parts=CAP)
        xT = r.take(KT, CAP)
        GUs = r.take(HID)
        Hs = r.take(4, CAP)
        HT = r.take(4, CAP)
        Os = r.take(2, 512)
        gfin = r.take(D)
        rt = Region(arena, r.at, 1024)
        mixT = Region(arena, at_c, SIZE_C).take(16, TO)
        hnT = Region(arena, at_c, SIZE_C).take(KT, TO)
        r = Region(arena, at_c, 8 * TO)
        lam_ld = r.take(2, 128, parts=NJ)
        st_ld = r.take(4, 128)
        b_ld = r.take(2, NJ * GC)
        prm = r.take(21, NJ)
        r = Region(arena, at_c + 8 * TO, 8 * TO)
        Bt = r.take(2, NJ, 16)
        At = r.take(2, NJ, 17)
        r = Region(arena, at_d, SIZE_D)
        eb = r.take(NCH, H, CL)
        en = r.take(NCH, H, CL)
        at_z = r.at
        zT = r.take(8, TO)
        at_S = r.at
        S = r.take(H, DV)
        BT = r.take(2, 8, 128)
        CT = r.take(2, 8, 128)
        at_m = r.at
        hl = r.take(2, 9, NJ)
        cmaskS = r.take(128)
        qmask = r.take(SPC, CL)
        s5mask = r.take(T)
        gmask8 = r.take(256)
        pad = Region(arena, at_z, 2560).take(2, 8, 128)
        c_ld = Region(arena, at_S, 1024).take(2, 8, P)
        r = Region(arena, at_d, 2816)
        P1, P2 = r.take(2, T), r.take(2, T)
        Gs = [r.take(2, T), r.take(2, T)]
        ets = Region(arena, at_d, 1344).take(4, 17, 16)
        hrow = Region(arena, at_d, 6144).take(3, D)
        hn = Region(arena, at_d + 6144, 6144).take(3, D)
        r = Region(arena, at_x, ARENA - at_x)
        ident = r.take(128)
        cmaskP = r.take(128)
        hmask = r.take(H)
        hsmask = r.take(H * SPC)
        gmix = r.take(KT)
        ggla, dsk, bgk, bglu = r.take(8), r.take(8), r.take(H), r.take(8)
        at_x2 = r.at
        Q1 = [r.take(2, T), r.take(2, T)]
        Q2 = r.take(2, T)
        dec = [r.take(T), r.take(T)]
        r = Region(arena, at_x2, 2688)
        Kexp = r.take(H * SPC, 128)
        Vn = [r.take(DV) for _ in range(2)]
        gffn = Region(arena, at_x2, 2688).take(D)
        hlT = Region(arena, at_x2, 2688).take(6, 128)
        r = Region(arena, at_m, SIZE_D + at_d - at_m)

        r = Region(arena, at_x2 + D, 640)
        Wr = r.take(KT, NG + NE)
        br = r.take(NG + NE)
        ssp = r.take(3, 8)
        wrg_ld = Region(arena, at_d + 6144, 64).take(KT, NG)
        wre_ld = Region(arena, at_d + 6208, 512).take(NG, KT, EPG)
        r = rt
        ewt = r.take(3, 2)
        dest = r.take(3, 2).bitcast(I32)
        ovexp = r.take(NOVF).bitcast(I32)
        novf = r.take(1).bitcast(I32)
        ssum = r.take(16)
        tri, ones = r.take(128), r.take(128)
        iota32 = r.take(NE)
        iota32i = r.take(NE).bitcast(I32)
        r = Region(arena, at_b + D + KT * CAP, 2048)
        Lg = r.take(3, NG + NE)
        lg8, gmx, gix, gidx = r.take(3, 8), r.take(3, 8), r.take(3, 8).bitcast(U32), r.take(3, 1)
        ohg, lem, lsel = r.take(3, NG), r.take(3, NG, EPG), r.take(3, 8)
        v8, ix8, eid = r.take(3, 8), r.take(3, 8).bitcast(U32), r.take(3, 2)
        M, M01, Mx = r.take(3, 2, NE), r.take(3, NE), r.take(3, 2, NE)
        x4, x1 = r.take(3, NG), r.take(3, 1)
        u2 = [r.take(3, 2) for _ in range(6)]
        u1 = [r.take(3, 1) for _ in range(6)]
        cnt, ov, ovc, t32 = r.take(NE), r.take(NE), r.take(NE), [r.take(NE), r.take(NE)]
        cmp9 = r.take(NOVF, NE)
        f9 = r.take(NOVF)
        hjunk = Region(arena, at_d + 6144 + 1024, 256).take(256)
        xss = Region(arena, at_g + 1024, 16).take(8)

        x_loaded0 = sem("x_loaded0")
        ring_loaded = [sem("ring_loaded0"), sem("ring_loaded1")]
        xn_sq, xn_sqrt, xn_rstd = sem("xn_sq"), sem("xn_sqrt"), sem("xn_rstd")
        filled = sem("filled")
        states_stored = sem("states_stored")
        small_loaded = sem("small_loaded")
        s5_loaded = sem("s5_loaded")
        ldt_loaded = sem("ldt_loaded")
        c_loaded = sem("c_loaded")
        masks_made = sem("masks_made")
        ident_made = sem("ident_made")
        pool_steps, act_steps, dve_steps = sem("pool_steps"), sem("act_steps"), sem("dve_steps")
        xn_scaled = sem("xn_scaled")
        xn_turned = sem("xn_turned")
        xn_ready = sem("xn_ready")
        prm_turned = sem("prm_turned")
        prm_ready = sem("prm_ready")
        h0_ready = sem("h0_ready")
        dt_ready = sem("dt_ready")
        arg_ready = sem("arg_ready")
        trig_ready = sem("trig_ready")
        tables_ready = sem("tables_ready")
        pad_ready = sem("pad_ready")
        pad_turned = sem("pad_turned")
        bt_ready, ct_ready = sem("bt_ready"), sem("ct_ready")
        proj_done = sem("proj_done")
        proj_read = sem("proj_read")
        bu_done = sem("bu_done")
        bu_read = sem("bu_read")
        dec_ready = sem("dec_ready")
        scanned = sem("scanned")
        rotated = sem("rotated")
        h_used = sem("h_used")
        hl_saved = sem("hl_saved")
        y_read = sem("y_read")
        z_ready = sem("z_ready")
        gk_ready = sem("gk_ready")
        gate_abs = sem("gate_abs")
        gate_b = sem("gate_b")
        gate_exp = sem("gate_exp")
        gates_ready = sem("gates_ready")
        ss_loaded = [sem("ss_loaded0"), sem("ss_loaded1")]
        front_done = sem("front_done")
        v_copied = sem("v_copied")
        front_ready = sem("front_ready")
        qexp_ready = sem("qexp_ready")
        o_done = sem("o_done")
        o_read = sem("o_read")
        st_done = sem("st_done")
        st_added = sem("st_added")
        o_sqrt = sem("o_sqrt")
        o_rstd = sem("o_rstd")
        o_scaled = sem("o_scaled")
        o_turned = sem("o_turned")
        mix_gla = sem("mix_gla")
        glu_sig = sem("glu_sig")
        mix_s5 = sem("mix_s5")
        stores = sem("stores")
        hl_turned = sem("hl_turned")
        hl_copied = sem("hl_copied")
        res_loaded = sem("res_loaded")
        wout_done = sem("wout_done")
        h_added = sem("h_added")
        ffn_loaded = sem("ffn_loaded")
        br_loaded = sem("br_loaded")
        wr_ready = sem("wr_ready")
        h_ss = sem("h_ss")
        h_rstd = sem("h_rstd")
        hn_ready = sem("hn_ready")
        hn_turned = sem("hn_turned")
        hnT_ready = sem("hnT_ready")
        logits_done = sem("logits_done")
        rconst = sem("rconst")
        ex_in, ex_out = sem("ex_in"), sem("ex_out")
        m_ready = sem("m_ready")
        rank_done = sem("rank_done")
        dest_ready = sem("dest_ready")
        zeroed = sem("zeroed")
        zero_tile = sem("zero_tile")
        scattered = sem("scattered")
        piece_loaded = [sem(f"piece_loaded{i}") for i in range(12)]
        weights_used = sem("weights_used")
        xrow_loaded = sem("xrow_loaded")
        x_turned = sem("x_turned")
        xT_a, xT_b = sem("xT_a"), sem("xT_b")
        gu_copied = sem("gu_copied")
        gu_turned = sem("gu_turned")
        silu_ready = sem("silu_ready")
        hid_ready = sem("hid_ready")
        out_a, out_b = sem("out_a"), sem("out_b")
        stored = sem("stored")
        gfin_loaded = sem("gfin_loaded")
        small_done = sem("small_done")
        fin_chain = [sem(f"fin_chain{t}") for t in range(3)]
        overflow_stored = sem("overflow_stored")
        experts_done = sem("experts_done")
        gathered = [sem(f"gathered{t}") for t in range(3)]
        fin_ss, fin_rstd, fin_ready = sem("fin_ss"), sem("fin_rstd"), sem("fin_ready")

        FILL = ((xg, 0), (yg, NE * CAP))
        NFILL = sum(-(-(NBLK * CAP - r0) // (2 * XT_ROWS)) for _, r0 in FILL)
        HALF = s5_half_steps()
        LATE = [HALF[j + 3] if j + 3 < NJ else HALF[-1] + 2 * (j + 4 - NJ) for j in range(NJ)]
        bu_at = {h: [j for j in range(NJ) if HALF[j] == h] for h in range(2 * len(TILES))}
        y_at = {h: [j for j in range(NJ) if LATE[j] == h] for h in range(2 * len(TILES))}
        TB = ((2, 3, 5, 6), (4, 7, 4, 7))
        YB = (4, 7)
        XB = (2, 3, 5, 6)
        OB = ((0, 1, 4), (5, 6, 7))
        FB = (5, 7)
        TR = [128, 128, 64]
        BU = [(2, 3), (5, 6)]
        (LR, LI, LDT, DT, X, TH, N_, R_, T1, T2, CARG, MAG, SI, CO, ABR, ABI, DEN, RDEN, FR, FI) = range(20)

        def pr(i):
            return prm[:, i, :]

        def st_count(c):
            return 2 * min(c, NCP) + 2 * SPC * max(c - NCP, 0)

        def h_last(ap):
            return ap[:, :, NPRE - 1:T:DSEQ]

        block = ctx.enter_context(nc.Block())

        def chunk_view(ap):
            return ap.rearrange("p h i -> p (h i)")

        @block.sync
        def _(sp):
            w_in = A["w_in"][0].rearrange("(p k) n -> p k n", k=KT)
            w_glu = A["w_glu"][0].rearrange("(k p) n -> p k n", p=128)
            w_out = A["w_out"][0].rearrange("(k p) n -> p k n", p=128)
            xp, xs = A["x_prompt"][0], A["x_sample"].rearrange("b t d -> (b t) d")

            def load_chunk(n):
                kind, i = CHUNKS[n]
                if n >= 2:
                    k0, i0 = CHUNKS[n - 2]
                    if k0 == "out":
                        sp.wait_ge(wout_done, 3 * (i0 + 1))
                    else:
                        sp.wait_ge(proj_done, TIDX[(k0, 2 * i0 + 1)] + 1)
                if kind == "glu":
                    src, dst = w_glu[:, :, 256 * i:256 * i + 256], ring[n % 2][:, 0:2048]
                elif kind == "out":
                    src, dst = w_out[:, :, 256 * i:256 * i + 256], ring[n % 2]
                else:
                    c0 = COL0[kind] + 256 * i
                    src, dst = w_in[:, :, c0:c0 + 256], ring[n % 2]
                sp.dma_start(dst.rearrange("p (k n) -> p k n", n=256), src).then_inc(ring_loaded[n % 2], 16)

            sp.dma_start(xr[0:N_META, 0, :], A["meta"]).then_inc(x_loaded0, 16)
            sp.dma_start(xr[N_META:XT_ROWS, 0, :], xp[0:96, :]).then_inc(x_loaded0, 16)
            sp.dma_start(xr[:, 1, :], xp[96:208, :]).then_inc(x_loaded0, 16)
            sp.dma_start(xr[0:48, 2, :], xp[208:256, :]).then_inc(x_loaded0, 16)
            sp.dma_start(xr[48:112, 2, :], xs).then_inc(x_loaded0, 16)
            load_chunk(0)
            load_chunk(1)
            sp.dma_start(lam_ld[:, 0, :], A["lam_re"][0].rearrange("(j g) p -> j (g p)", g=2)).then_inc(s5_loaded, 16)
            sp.dma_start(lam_ld[:, 1, :], A["lam_im"][0].rearrange("(j g) p -> j (g p)", g=2)).then_inc(s5_loaded, 16)
            for r_, name in enumerate(("state_s5_re", "state_s5_im")):
                src = A[name][0].rearrange("b (j g) p -> (b j) (g p)", g=2)
                for m in range(2):
                    sp.dma_start(st_ld[:, 2 * r_ + m, :], src[128 * m:128 * m + 128, :]).then_inc(s5_loaded, 16)
            for r_, name in enumerate(("s5_b_re", "s5_b_im")):
                src = A[name][0].rearrange("(j g) p c -> (g p) j c", g=2)
                sp.dma_start(b_ld[:, r_, :].rearrange("p (j c) -> p j c", c=GC), src).then_inc(s5_loaded, 16)
            for r_, name in enumerate(("s5_c_re", "s5_c_im")):
                src = A[name][0].rearrange("(c g) x p -> (g x) c p", g=8)
                sp.dma_start(c_ld[:, r_], src).then_inc(c_loaded, 16)
            sp.wait_ge(xn_scaled, 3)
            for dst, r0 in FILL:
                for r_ in range(r0, NBLK * CAP, 2 * XT_ROWS):
                    n = min(XT_ROWS, (NBLK * CAP - r_) // 2)
                    sp.dma_start(dst[r_:r_ + 2 * n, :].rearrange("(p t) d -> p t d", t=2), xr[0:n, 0:2, :])\
                      .then_inc(filled, 16)
            for n in range(2, CIDX[("out", 2)]):
                load_chunk(n)
                if n == CIDX[("r", 0)]:
                    sp.wait_ge(rotated, 2 * NJ)
                    for s_ in range(SPC):
                        sp.dma_start(sstate[0][:, s_], A["state_gla"][0, s_].rearrange("h k v -> k h v"))\
                          .then_inc(ss_loaded[0], 16)
                if n == CIDX[("glu", 2)]:
                    sp.wait_ge(proj_done, TIDX[("glu", 0)])
                    for s_ in range(SPC):
                        sp.dma_start(sstate[1][:, s_], A["state_gla"][0, SPC + s_].rearrange("h k v -> k h v"))\
                          .then_inc(ss_loaded[1], 16)

            def expert_weights(e, first, pieces):
                for j in pieces:
                    if j < 8:
                        name, q, kt, n = ("w_gate", "w_up")[j % 2], j // 2, KT, HID
                    else:
                        name, q, kt, n = "w_down", j - 8, HID // 128, D
                    per = 2048 // n
                    src = A[name][0].rearrange("e (p k) n -> e p (k n)", k=kt)
                    if first is not None:
                        sp.wait_ge(weights_used, 12 * first + j - 11)
                    sp.dma_start(wpiece[j], src[bass.ds(e, 1), :, per * q * n:per * (q + 1) * n]
                                 .rearrange("e p n -> (e p) n")).then_inc(piece_loaded[j], 16)

            sp.wait_ge(mix_gla, 2 * (NCH - 1))
            sp.wait_ge(states_stored, 16 * (2 * NSEQ + H))
            expert_weights(0, None, range(4))
            for i in range(2, 8):
                load_chunk(CIDX[("out", i)])
                if i < 4:
                    expert_weights(0, None, range(4 * i - 4, 4 * i))
            sp.wait_ge(scattered, 96)

            def x_rows(n):
                sp.dma_start(xrow, xg[bass.ds(n * CAP, CAP), :]).then_inc(xrow_loaded, 16)

            x_rows(0)
            with sp.Fori(1, NE) as e:
                sp.wait_ge(x_turned, 2 * e)
                x_rows(e)
                expert_weights(e, e, range(12))
            n_over = sp.value_load(novf[0:1, 0:1], min_val=0, max_val=NOVF)
            with sp.Fori(0, NOVF) as o:
                with sp.If(n_over > o):
                    e = sp.value_load(ovexp[0:1, bass.ds(o, 1)], min_val=0, max_val=NE - 1)
                    sp.wait_ge(x_turned, 2 * (o + NE))
                    x_rows(o + NE)
                    expert_weights(e, o + NE, range(12))
                sp.nop()

        @block.gpsimd
        def _(pool):
            gp = nc.gpsimd
            st = Steps(pool, pool_steps)

            def keep(ap, pattern, base, mult, count=masks_made):
                st.sync()
                return gp.affine_select(out=ap, in_=ap, compare_op=ALU.is_ge, fill=0.0, base=base,
                                        pattern=pattern, channel_multiplier=mult)

            st(gp.memset(ident, 1.0))
            st(keep(ident, [[-1, 128]], 0, 1))
            st.sync()
            keep(ident, [[1, 128]], 0, -1).then_inc(ident_made, 1)
            with nc.allow_non_contiguous_dma(reason="short per-channel vectors"):
                vecs = [
                    (gmix, A["g_mix"][0].rearrange("(p k) -> p k", k=KT)),
                    (ggla, A["g_gla"][0].rearrange("h (m p) -> p (h m)", p=128)),
                    (dsk, A["d_skip"][0].rearrange("(c g) x -> (g x) c", g=8)),
                    (bgk, A["b_gk"][0].rearrange("(h p) -> p h", p=128)),
                    (bglu, A["b_glu"][0].rearrange("(c p) -> p c", p=128)),
                    (wgk, A["w_gk2"][0]),
                    (wa, A["w_in"][0].rearrange("(p k) n -> p k n", k=KT)[:, :, OFF_A:OFF_A + RANK]),
                ]
                ldt = A["log_dt"][0].rearrange("(j g) -> g j", g=2)
                for g2 in range(2):
                    pool.dma_start(prm[64 * g2:64 * g2 + 64, LDT, :], ldt[g2:g2 + 1, :].broadcast_to([64, NJ]))\
                        .then_inc(ldt_loaded, 16)
                for dst, src in vecs:
                    pool.dma_start(dst, src).then_inc(small_loaded, 16)
            for m, w in ((cmaskP, CL), (cmaskS, DSEQ)):
                st(gp.memset(m, 1.0))
                st(keep(m, [[1, 128]], 0, -1))
                st(keep(m, [[-w, 128 // w], [0, w]], 0, 1))
            for m, w in ((hmask, CL), (hsmask, DSEQ)):
                st(gp.memset(m, 1.0))
                st(keep(m, [[-w, 128 // w]], 0, 1))
                st(keep(m, [[w, 128 // w]], w - 1, -1))
            st(gp.memset(qmask, 1.0))
            st(keep(qmask, [[-DSEQ, SPC], [1, CL]], 0, 0))
            st(keep(qmask, [[DSEQ, SPC], [-1, CL]], DSEQ - 1, 0))
            st(gp.memset(s5mask, 1.0))
            st(gp.memset(gmask32, 1.0))
            st(gp.memset(gmask8, 1.0))
            st.sync()
            st(gp.memset(s5mask[:, 0:1], 0.0))
            st(gp.memset(s5mask[:, NPRE:T:DSEQ], 0.0))
            st(gp.memset(gmask32[:, 0:384:CL], 0.0))
            st(gp.memset(gmask8[:, 0:256:DSEQ], 0.0))
            m8 = prm[:, 20, 0:8]
            par = prm[:, 20, 8:10]
            st(gp.memset(m8, 1.0))
            st(keep(m8, [[-GC, 8]], 0, 1))
            st(keep(m8, [[GC, 8]], GC - 1, -1))
            st.sync()
            p4 = prm[:, 20, 10:14]
            m8v = m8.rearrange("p (a g) -> p a g", g=2)
            st(gp.tensor_tensor(p4.rearrange("p (a g) -> p a g", g=2), m8v[:, 0:2], m8v[:, 2:4], ALU.add))
            st.sync()
            st(gp.tensor_tensor(par, p4[:, 0:2], p4[:, 2:4], ALU.add))
            for m in (qT, kT):
                st(gp.memset(m[:, 0, :, 0:PADT], 0.0))
            st(gp.memset(pad, 0.0))
            st.sync()
            pool.sem_inc(masks_made, 1)

            def mul(o, a, b):
                st(gp.tensor_tensor(o, a, b, ALU.mult))

            def add(o, a, b):
                st(gp.tensor_tensor(o, a, b, ALU.add))

            def sub(o, a, b):
                st(gp.tensor_tensor(o, a, b, ALU.subtract))

            pool.wait_ge(prm_ready, 1)
            pool.wait_ge(dt_ready, 1)
            mul(pr(X), pr(LR), pr(DT))
            mul(pr(TH), pr(LI), pr(DT))
            mul(pr(T1), pr(LR), pr(LR))
            mul(pr(T2), pr(LI), pr(LI))
            st.sync()
            gp.tensor_tensor(pr(DEN), pr(T1), pr(T2), ALU.add).then_inc(arg_ready, 1)
            st(gp.tensor_scalar(pr(N_), pr(TH), 1.0 / (2 * math.pi), MAGIC, ALU.mult, ALU.add))
            st.sync()
            st(gp.tensor_scalar(pr(N_), pr(N_), -MAGIC, None, ALU.add))
            st.sync()
            st(gp.tensor_scalar(pr(T1), pr(N_), TWO_PI_1, None, ALU.mult))
            st(gp.tensor_scalar(pr(T2), pr(N_), TWO_PI_2, None, ALU.mult))
            st.sync()
            sub(pr(R_), pr(TH), pr(T1))
            st.sync()
            st(gp.tensor_scalar(pr(T1), pr(N_), TWO_PI_3, None, ALU.mult))
            sub(pr(R_), pr(R_), pr(T2))
            st.sync()
            sub(pr(R_), pr(R_), pr(T1))
            st.sync()
            st(gp.tensor_scalar(pr(R_), pr(R_), 3.1415925, -3.1415925, ALU.min, ALU.max))
            st.sync()
            st(gp.tensor_scalar(pr(T1), pr(R_), 0.0, None, ALU.min))
            st(gp.tensor_scalar(pr(T2), pr(R_), 0.0, None, ALU.max))
            st.sync()
            sub(pr(T2), pr(T2), pr(T1))
            st.sync()
            gp.tensor_scalar(pr(CARG), pr(T2), -1.0, math.pi / 2, ALU.mult, ALU.add).then_inc(arg_ready, 1)
            pool.wait_ge(trig_ready, 3)
            mul(pr(ABR), pr(MAG), pr(CO))
            mul(pr(ABI), pr(MAG), pr(SI))
            st.sync()
            st(gp.tensor_scalar(pr(N_), pr(ABR), -1.0, None, ALU.add))
            mul(pr(T2), pr(ABI), pr(LI))
            mul(pr(FI), pr(ABI), pr(LR))
            st.sync()
            mul(pr(T1), pr(N_), pr(LR))
            mul(pr(FR), pr(N_), pr(LI))
            st.sync()
            sub(pr(FI), pr(FI), pr(FR))
            add(pr(T1), pr(T1), pr(T2))
            st.sync()
            pool.wait_ge(dt_ready, 2)
            mul(pr(FI), pr(FI), pr(RDEN))
            mul(pr(FR), pr(T1), pr(RDEN))
            st.sync()
            pool.wait_ge(s5_loaded, 16 * 8)
            tb = Region(arena, at_d + 1344 + 16, 1456)
            ta, tc = tb.take(NJ, GC), tb.take(NJ, GC)
            bv = [b_ld[:, r_, :].rearrange("p (j c) -> p j c", c=GC) for r_ in range(2)]
            fr, fi = (bc(pr(x).unsqueeze(2), 2, GC) for x in (FR, FI))
            for r_ in range(2):
                st.sync()
                mul(ta, fr, bv[r_])
                mul(tc, fi, bv[1 - r_])
                st.sync()
                padv = pad[:, r_].rearrange("p c (q g x) -> p (c q) g x", q=4, g=2)
                for g2 in range(2):
                    rows = slice(64 * g2, 64 * g2 + 64)
                    st(gp.tensor_tensor(padv[rows, :, g2, :], ta[rows], tc[rows], ALU.subtract if r_ == 0 else ALU.add))
            st.sync()
            pool.sem_inc(pad_ready, 1)
            pool.wait_ge(h0_ready, 1)
            tA, tB = (x.rearrange("p j c -> p (j c)")[:, 0:NSEQ * NJ].rearrange("p (b j) -> p b j", b=NSEQ) for x in (ta, tc))
            ar, ai = (bc(pr(x).unsqueeze(1), 1, NSEQ) for x in (ABR, ABI))
            for r_ in range(2):
                st.sync()
                mul(tA, ar, h0[:, r_])
                mul(tB, ai, h0[:, 1 - r_])
                st.sync()
                st(gp.tensor_tensor(ah0[:, r_].rearrange("p j b -> p b j"), tA, tB, ALU.subtract if r_ == 0 else ALU.add))
            tw = [x.rearrange("p j c -> p (j c)")[:, 256 * i:256 * i + 256] for x in (ta, tc) for i in range(2)]

            def cmul(o, a, e, w):
                t = [x[:, 0:NJ * w].rearrange("p (j w) -> p j w", w=w) for x in tw]
                er, ei = (bc(x.unsqueeze(2), 2, w) for x in e)
                st.sync()
                mul(t[0], a[0], er)
                mul(t[1], a[1], ei)
                mul(t[2], a[0], ei)
                mul(t[3], a[1], er)
                st.sync()
                sub(o[0], t[0], t[1])
                add(o[1], t[2], t[3])

            def cols(tab, a, b):
                return tab[:, 0, :, a:b], tab[:, 1, :, a:b]

            for tab in (Bt, At):
                st(gp.memset(tab[:, 0, :, 0:1], 1.0))
                st(gp.memset(tab[:, 1, :, 0:1], 0.0))
            e = (pr(CO), pr(SI))
            e2 = [(pr(T1), pr(T2)), (pr(X), pr(TH))]
            st.sync()
            st(gp.tensor_copy(Bt[:, 0, :, 1:2], e[0].unsqueeze(2)))
            st(gp.tensor_copy(Bt[:, 1, :, 1:2], e[1].unsqueeze(2)))
            for lvl, (tab, w) in enumerate([(Bt, 2), (Bt, 4), (Bt, 8), (At, 1), (At, 2), (At, 4), (At, 8), (At, 16)]):
                n = e2[lvl % 2]
                cmul(tuple(x.unsqueeze(2) for x in n), tuple(x.unsqueeze(2) for x in e), e, 1)
                e = n
                hi = min(2 * w, tab.shape[3])
                cmul(cols(tab, w, hi), cols(tab, 0, hi - w), e, hi - w)
            st.sync()
            pool.sem_inc(tables_ready, 1)
            pool.wait_ge(c_loaded, 32)
            pool.wait_ge(pad_turned, 4)
            for r_ in range(2):
                pv = pad[:, r_].rearrange("p c (g x) -> p c g x", g=2)
                for g2 in range(2):
                    st(gp.tensor_scalar(pv[:, :, g2, :], c_ld[:, r_], par[:, g2:g2 + 1], 1.0 if r_ == 0 else -1.0,
                                        ALU.mult, ALU.mult))
            st.sync()
            pool.sem_inc(pad_ready, 1)

            pool.wait_ge(filled, 16 * NFILL)
            for hf in range(2):
                st(gp.memset(vT[:, hf, 0, :].rearrange("p (h i) -> p h i", i=CL)[:, :, 0:PADT], 0.0))
            st.sync()
            pool.sem_inc(masks_made, 1)

            for j in range(NJ):
                c, q = j // 4, j % 4
                cs, sn = (bc(E[c % 2][:, r_:r_ + 1, q, :], 1, 2) for r_ in range(2))
                g_, q1 = Gs[j % 2], Q1[j % 2]
                pool.wait_ge(scanned, 2 * (j + 1))
                if j >= 2:
                    pool.wait_ge(h_used, j - 1)
                    pool.wait_ge(hl_saved, j - 1)
                if j:
                    pool.wait_ge(rotated, 2 * j)
                st.sync()
                mul(q1, cs, g_)
                mul(Q2, sn, g_)
                st.sync()
                gp.tensor_tensor(q1[:, 0], q1[:, 0], Q2[:, 1], ALU.subtract).then_inc(rotated, 1)
                gp.tensor_tensor(q1[:, 1], q1[:, 1], Q2[:, 0], ALU.add).then_inc(rotated, 1)
            pool.wait_ge(pad_turned, 8)
            gp.memset(S, 0.0).then_inc(masks_made, 1)
            pool.wait_ge(hl_copied, 2)
            for r_, name in enumerate(("re", "im")):
                pool.dma_start(A[f"new_s5_{name}_prompt"].rearrange("l b (j g) p -> (l b j) (g p)", g=2),
                               hlT[0:NJ, 3 * r_, :]).then_inc(stores, 16)
                dst = A[f"new_s5_{name}_sample"].rearrange("l b (j g) p -> (l b j) (g p)", g=2)
                for m in range(2):
                    pool.dma_start(dst[128 * m:128 * m + 128, :], hlT[:, 3 * r_ + 1 + m, :]).then_inc(stores, 16)
            pool.wait_ge(st_added, 2 * st_count(NCH))
            for h_ in range(H):
                pool.dma_start(A["new_gla_prompt"][0, 0, h_], S[:, h_]).then_inc(states_stored, 16)
            for s_ in range(NSEQ):
                for hp in range(2):
                    pool.dma_start(A["new_gla_sample"][0, s_, 2 * hp:2 * hp + 2].rearrange("h k v -> k h v"),
                                   sstate[s_ // SPC][:, s_ % SPC, 2 * hp:2 * hp + 2]).then_inc(states_stored, 16)
            pool.wait_ge(states_stored, 16 * (2 * NSEQ + H))
            pool.wait_ge(stores, 6 * 16)
            pool.wait_ge(mix_s5, 8)
            pool.wait_ge(mix_gla, 2 * (NCH - 1))
            pool.dma_start(hrow[:, 0, :], A["x_prompt"][0, 0:128, :]).then_inc(res_loaded, 16)
            pool.dma_start(hrow[:, 1, :], A["x_prompt"][0, 128:256, :]).then_inc(res_loaded, 16)
            pool.dma_start(hrow[0:NS, 2, :], A["x_sample"].rearrange("b t d -> (b t) d")).then_inc(res_loaded, 16)
            pool.dma_start(gffn, A["g_ffn"].broadcast_to([128, D])).then_inc(ffn_loaded, 16)
            pool.dma_start(wrg_ld, A["w_rg"][0].rearrange("(p k) g -> p k g", k=KT)).then_inc(ffn_loaded, 16)
            pool.dma_start(wre_ld, A["w_re"][0].rearrange("g (p k) e -> p g k e", k=KT)).then_inc(ffn_loaded, 16)
            pool.dma_start(br[:, 0:NG], A["b_rg"].broadcast_to([128, NG])).then_inc(ffn_loaded, 16)
            pool.dma_start(br[:, NG:], A["b_re"].rearrange("l g e -> l (g e)").broadcast_to([128, NE])).then_inc(ffn_loaded, 16)
            pool.wait_ge(ffn_loaded, 80)
            gp.tensor_copy(Wr[:, :, 0:NG], wrg_ld).then_inc(wr_ready, 1)
            for g_ in range(NG):
                gp.tensor_copy(Wr[:, :, NG + EPG * g_:NG + EPG * g_ + EPG], wre_ld[:, g_]).then_inc(wr_ready, 1)
            pool.wait_ge(wout_done, 24)
            pool.dma_start(gfin, A["g_final"].rearrange("(a d) -> a d", a=1).broadcast_to([128, D])).then_inc(gfin_loaded, 16)
            st(gp.memset(ones, 1.0))
            st(gp.memset(tri, 1.0))
            st(gp.memset(Lg, 0.0))
            st(gp.memset(lg8, -BIG))
            st(gp.memset(ssum, 1.0))
            st.sync()
            st(gp.affine_select(out=tri, in_=tri, compare_op=ALU.is_ge, fill=0.0, base=-1, pattern=[[1, 128]],
                                channel_multiplier=-1))
            st(gp.iota(iota32i, pattern=[[1, NE]], base=0, channel_multiplier=0))
            st.sync()
            st(gp.tensor_copy(iota32, iota32i))
            st.sync()
            pool.sem_inc(rconst, 1)
            pool.wait_ge(dest_ready, 1)
            pool.wait_ge(filled, 16 * NFILL)
            for t in range(3):
                for k in range(2):
                    pool.indirect_dma_start(out=xg, out_offset=bass.IndirectOffsetOnAxis(ap=dest[0:TR[t], t, k:k + 1], axis=0),
                                            in_=hn[0:TR[t], t, :], in_offset=None).then_inc(scattered, 16)
            pool.wait_ge(experts_done, 1)
            for t in range(3):
                for k in range(2):
                    pool.indirect_dma_start(out=yrows[2 * t + k][0:TR[t], :], out_offset=None, in_=yg,
                                            in_offset=bass.IndirectOffsetOnAxis(ap=dest[0:TR[t], t, k:k + 1], axis=0))\
                        .then_inc(gathered[t], 16)
            outs = [A["y_prompt"][0, 0:128, :], A["y_prompt"][0, 128:256, :], A["y_sample"].rearrange("b t d -> (b t) d")]
            for t in range(3):
                pool.wait_ge(fin_ready, t + 1)
                pool.dma_start(outs[t], hn[0:TR[t], t, :]).then_inc(stores, 16)
            pool.wait_ge(stores, 9 * 16)

        @block.scalar
        def _(act):
            sc = nc.scalar
            st = Steps(act, act_steps)
            act.wait_ge(x_loaded0, 80)
            for t in range(3):
                ejunk = arena[0:XT_ROWS, D * t:D * t + D]
                sc.activation(ejunk, xr[:, t, :], ACT.Square, accum_out=xss[0:XT_ROWS, t:t + 1]).then_inc(xn_sq, 1)
            act.wait_ge(xn_sq, 4)
            sc.activation(xss[0:XT_ROWS, 0:3], xss[0:XT_ROWS, 0:3], ACT.Sqrt).then_inc(xn_sqrt, 1)
            act.wait_ge(xn_rstd, 1)
            for t in range(3):
                sc.activation(xr[:, t, :], xr[:, t, :], ACT.Copy, scale=xss[0:XT_ROWS, 4 + t:5 + t]).then_inc(xn_scaled, 1)
            act.wait_ge(ldt_loaded, 32)
            act.wait_ge(prm_turned, 1)
            sc.activation(prm[:, LR:LI + 1, :], ps[:, 4, 0:2 * NJ].rearrange("p (a j) -> p a j", a=2), ACT.Copy)\
              .then_inc(prm_ready, 1)
            sc.activation(pr(DT), pr(LDT), ACT.Exp).then_inc(dt_ready, 1)
            act.wait_ge(prm_turned, 2)
            act.wait_ge(xn_turned, 12)
            sc.activation(h0.rearrange("p r b j -> p (r b j)"), ps[:, 7, :], ACT.Copy).then_inc(h0_ready, 1)
            act.wait_ge(arg_ready, 2)
            sc.activation(pr(MAG), pr(X), ACT.Exp).then_inc(trig_ready, 1)
            sc.activation(pr(SI), pr(R_), ACT.Sin).then_inc(trig_ready, 1)
            sc.activation(pr(CO), pr(CARG), ACT.Sin).then_inc(trig_ready, 1)

            def turn_copies(k):
                dst = (BT, CT)[k]
                for i in range(4):
                    act.wait_ge(pad_turned, 4 * k + i + 1)
                    out = dst[:, i // 2, 4 * (i % 2):4 * (i % 2) + 4, :].rearrange("p c x -> p (c x)")
                    sc.activation(out, ps[:, TB[k][i], :], ACT.Copy).then_inc((bt_ready, ct_ready)[k], 1)

            def decay(j):
                if j == 0:
                    act.wait_ge(trig_ready, 3)
                    act.wait_ge(masks_made, 1)
                if j >= 2:
                    act.wait_ge(scanned, 2 * (j - 1))
                sc.activation(dec[j % 2], s5mask, ACT.Copy, scale=prm[:, MAG, j:j + 1]).then_inc(dec_ready, 1)

            def keep_last(j):
                act.wait_ge(rotated, 2 * (j + 1))
                sc.activation(hl[:, :, :, j], h_last(Q1[j % 2]), ACT.Copy).then_inc(hl_saved, 1)

            def evacuate(p):
                kind, i = TILES[p]
                act.wait_ge(proj_done, p + 1)
                src = ps[:, p % 2, 0:T]
                if kind == "u":
                    sc.activation(uT[:, i, :], src, ACT.Copy).then_inc(proj_read, 1)
                elif kind == "a":
                    act.wait_ge(xn_turned, 12)
                    sc.activation(aT, ps[0:RANK, p % 2, 0:T], ACT.Copy).then_inc(proj_read, 1)
                elif kind in "qkv":
                    if kind == "v" and i == 0:
                        act.wait_ge(filled, 16 * NFILL)
                    if kind == "v":
                        h_, dst = i // 2, vT[:, i % 2].rearrange("p c (h i) -> p c h i", i=CL)
                    else:
                        h_, dst = i, qT if kind == "q" else kT
                    scale = DK ** -0.5 if kind == "q" else 1.0
                    st(sc.activation(dst[:, 0, h_, PADT:CL], src[:, 0:N_META], ACT.Copy, scale=scale))
                    sc.activation(dst[:, 1:, h_, :], src[:, N_META:].rearrange("p (c i) -> p c i", i=CL), ACT.Copy,
                                  scale=scale).then_inc(proj_read, 1)
                elif kind == "gk":
                    act.wait_ge(scanned, 2 * NJ)
                    st(sc.activation(bG[:, 0, i, PADT:CL], src[:, 0:N_META], ACT.Identity, bias=bgk[:, i:i + 1]))
                    sc.activation(bG[:, 1:, i, :], src[:, N_META:].rearrange("p (c i) -> p c i", i=CL), ACT.Identity,
                                  bias=bgk[:, i:i + 1]).then_inc(proj_read, 1)
                elif kind == "r":
                    sc.activation(rT[:, i, :], src[:, 0:TO], ACT.Silu).then_inc(proj_read, 1)
                else:
                    if i >= 2:
                        act.wait_ge(mix_s5, i - 1)
                    sc.activation(glu_t[i % 2], src[:, 0:TO], ACT.Sigmoid, bias=bglu[:, i:i + 1]).then_inc(proj_read, 1)

            def gates():
                act.wait_ge(rotated, 2 * NJ)
                act.wait_ge(proj_read, TIDX[("gk", 3)] + 1)
                act.wait_ge(gate_b, 1)
                flat = [x.rearrange("p c h i -> p (c h i)") for x in (bG, eb, en)]
                sc.activation(flat[2], flat[0], ACT.Abs).then_inc(gate_abs, 1)
                act.wait_ge(gate_abs, 1)
                sc.activation(flat[2], flat[2], ACT.Exp, scale=-1.0).then_inc(gate_abs, 1)
                act.wait_ge(gate_abs, 2)
                sc.activation(flat[2], flat[2], ACT.Ln, bias=1.0).then_inc(gate_abs, 1)
                act.wait_ge(gate_b, 3)
                sc.activation(flat[1], flat[0], ACT.Exp, scale=1.0 / 16).then_inc(gate_exp, 1)
                sc.activation(flat[2], flat[2], ACT.Exp, scale=-1.0 / 16).then_inc(gate_exp, 1)
                act.wait_ge(gate_b, 5)
                sc.activation(flat[0], flat[0], ACT.Exp, scale=1.0 / 16).then_inc(gate_exp, 1)

            def copy_v(c):
                act.wait_ge(front_done, c + 1)
                if c >= 2:
                    act.wait_ge(st_done, st_count(c - 1))
                sc.activation(Vn[c % 2], ps[:, 4, 0:DV], ACT.Copy).then_inc(v_copied, 1)

            def read_o(c):
                if c >= 1:
                    act.wait_ge(o_done, c)
                    st(sc.activation(junk, ps[:, 6, 0:DV], ACT.Square, accum_out=gss[:, c - 1:c]))
                    sc.activation(o_all[:, c - 1, :], ps[:, 6, 0:DV], ACT.Copy).then_inc(o_read, 1)

            for p in range(len(TILES)):
                if p == 2:
                    turn_copies(0)
                if p == 4:
                    turn_copies(1)
                for h_ in (2 * p, 2 * p + 1):
                    for j in bu_at[h_]:
                        decay(j)
                    for j in y_at[h_]:
                        keep_last(j)
                if p == TIDX[("glu", 0)]:
                    act.wait_ge(y_read, 8)
                    sc.activation(zT.rearrange("p c t -> p (c t)"), zT.rearrange("p c t -> p (c t)"),
                                  ACT.Gelu_apprx_tanh).then_inc(z_ready, 1)
                c = p - GLA_TILE0
                if 0 <= c < NCH:
                    copy_v(c)
                evacuate(p)
                if TILES[p] == ("gk", 3):
                    gates()
                if 0 <= c < NCH:
                    read_o(c)
            for c in range(len(TILES) - GLA_TILE0, NCH):
                copy_v(c)
                read_o(c)
            act.wait_ge(o_sqrt, 1)
            sc.activation(gss[:, 0:NCH - 1], gss[:, 0:NCH - 1], ACT.Sqrt).then_inc(o_sqrt, 1)
            act.wait_ge(o_rstd, 1)
            for c in range(NCH - 1):
                sc.activation(o_all[:, c, :], o_all[:, c, :], ACT.Copy, scale=gss[:, 16 + c:17 + c]).then_inc(o_scaled, 1)
            for i in range(2):
                act.wait_ge(hl_turned, i + 1)
                sc.activation(hlT[:, 3 * i:3 * i + 3, :], ps[:, 2 + i, 0:384].rearrange("p (a b) -> p a b", b=128),
                              ACT.Copy).then_inc(hl_copied, 1)
            for i in range(8):
                for t in range(3):
                    act.wait_ge(h_added, 3 * i + t + 1)
                    if 3 * i + t:
                        act.wait_ge(h_ss, 3 * i + t)
                    sc.activation(hjunk[0:TR[t]], hrow[0:TR[t], t, 256 * i:256 * i + 256], ACT.Square,
                                  accum_out=ssp[0:TR[t], t, i:i + 1]).then_inc(h_ss, 1)
            act.wait_ge(h_rstd, 1)
            sc.activation(ssum[:, 0:3], ssum[:, 0:3], ACT.Sqrt).then_inc(h_rstd, 1)
            for n in range(12):
                t, g_ = n // 4, n % 4
                act.wait_ge(hn_turned, n + 1)
                sc.activation(hnT[:, 4 * g_:4 * g_ + 4, 128 * t:128 * t + TR[t]],
                              ps[:, XB[n % 4], 0:4 * TR[t]].rearrange("p (k t) -> p k t", k=4), ACT.Copy).then_inc(hnT_ready, 1)
            for i in range(2):
                act.wait_ge(ex_in, i + 1)
                x_ = (x4.rearrange("p t g -> p (t g)"), x1.rearrange("p t g -> p (t g)"))[i]
                sc.activation(x_, x_, ACT.Exp).then_inc(ex_out, 1)

            def expert(n, first=False):
                act.wait_ge(x_turned, 2 * n + 1)
                sc.activation(xT[:, 0:8].rearrange("p k t -> p (k t)"), ps[:, 2, :], ACT.Copy).then_inc(xT_a, 1)
                act.wait_ge(gu_turned, n + 1)
                gt = ps[:, 1, :].rearrange("p (k x t) -> p k x t", k=4, x=2)
                sc.activation(Hs, gt[:, :, 0, :], ACT.Silu).then_inc(silu_ready, 1)
                act.wait_ge(weights_used, 12 * (n + 1))
                if not first:
                    act.wait_ge(stored, 32 * n)
                sc.activation(Os[:, 0, :], ps[:, 6, :], ACT.Copy).then_inc(out_a, 1)
                act.wait_ge(out_a, n + 1)
                act.wait_ge(out_b, n + 1)
                rows = yg[bass.ds(n * CAP, CAP), :].rearrange("s (j x c) -> x s j c", j=2, x=2)
                for x in range(2):
                    act.dma_start(rows[x], Os[CAP * x:CAP * x + CAP]).then_inc(stored, 16)

            act.wait_ge(small_done, 1)
            expert(0, True)
            with act.Fori(1, NE) as e:
                expert(e)
            n_over = act.value_load(novf[0:1, 0:1], min_val=0, max_val=NOVF)
            act.wait_ge(stored, 32 * NE)
            with act.Fori(0, NOVF) as o:
                with act.If(n_over > o):
                    expert(o + NE)
                    act.wait_ge(stored, 32 * (o + NE + 1))
                    act.sem_inc(overflow_stored, 1)
                act.nop()
            act.sem_inc(experts_done, 1)
            for t in range(3):
                act.wait_ge(fin_ss, 2 * t + 1)
                sc.activation(hn[0:TR[t], t, :], hrow[0:TR[t], t, :], ACT.Square, accum_out=ssum[0:TR[t], 8 + t:9 + t])\
                  .then_inc(fin_rstd, 1)
                act.wait_ge(fin_ss, 2 * t + 2)
                sc.activation(ssum[0:TR[t], 8 + t:9 + t], ssum[0:TR[t], 8 + t:9 + t], ACT.Sqrt).then_inc(fin_rstd, 1)

        @block.vector
        def _(dve):
            ve = nc.vector
            st = Steps(dve, dve_steps)
            dve.wait_ge(xn_sq, 3)
            v3 = xss[0:XT_ROWS, 0:3]
            ve.tensor_scalar(v3, v3, 1.0 / D, EPS, ALU.mult, ALU.add).then_inc(xn_sq, 1)
            dve.wait_ge(xn_sqrt, 1)
            ve.reciprocal(xss[0:XT_ROWS, 4:7], v3).then_inc(xn_rstd, 1)
            dve.wait_ge(small_loaded, 7 * 16)
            for n in range(12):
                t, g = n // 4, n % 4
                dve.wait_ge(xn_turned, n + 1)
                ve.tensor_tensor(xnT[:, 4 * g:4 * g + 4, XT_ROWS * t:XT_ROWS * t + XT_ROWS],
                                 ps[:, XB[n % 4], 0:4 * XT_ROWS].rearrange("p (k t) -> p k t", k=4),
                                 bc(gmix[:, 4 * g:4 * g + 4].unsqueeze(2), 2, XT_ROWS), ALU.mult).then_inc(xn_ready, 1)
            dve.wait_ge(arg_ready, 1)
            ve.reciprocal(pr(RDEN), pr(DEN)).then_inc(dt_ready, 1)

            def tables(c):
                e = E[c % 2]
                if c >= 2:
                    dve.wait_ge(rotated, 8 * (c - 1))
                a = [bc(At[:, r_, 4 * c:4 * c + 4, :].unsqueeze(3), 3, 16) for r_ in range(2)]
                b = [bc(Bt[:, r_, 4 * c:4 * c + 4, :].unsqueeze(2), 2, 17) for r_ in range(2)]
                if c:
                    dve.wait_ge(scanned, 8 * c - 4)
                    st.sync()
                ev = [e[:, r_, :, 0:NPRE].rearrange("p j (a b) -> p j a b", b=16) for r_ in range(2)]
                for r_, (x, y, op) in enumerate(((1, 1, ALU.subtract), (1, 0, ALU.add))):
                    st(ve.tensor_tensor(ev[r_], a[0], b[0 if r_ == 0 else 1], ALU.mult))
                    st(ve.tensor_tensor(ets, a[x], b[y], ALU.mult))
                    st.sync()
                    st(ve.tensor_tensor(ev[r_], ev[r_], ets, op))
                    st.sync()
                for r_ in range(2):
                    st(ve.tensor_copy(e[:, r_, :, NPRE:T].rearrange("p j (s t) -> p j s t", t=DSEQ),
                                      bc(e[:, r_, :, 0:DSEQ].unsqueeze(2), 2, NSEQ)))
                st.sync()

            def forward(j):
                c, q = j // 4, j % 4
                cs, sn = (bc(E[c % 2][:, r_:r_ + 1, q, :], 1, 2) for r_ in range(2))
                bu = ps[:, BU[j % 2][0]:BU[j % 2][1] + 1, 0:T]
                if j:
                    dve.wait_ge(scanned, 2 * j)
                st.sync()
                dve.wait_ge(bu_done, 2 * (j + 1))
                st(ve.tensor_tensor(P1, cs, bu, ALU.mult))
                ve.tensor_tensor(P2, sn, bu, ALU.mult).then_inc(bu_read, 1)
                st.sync()
                dve.wait_ge(bu_read, j + 1)
                st(ve.tensor_tensor(P1[:, 0], P1[:, 0], P2[:, 1], ALU.add))
                st(ve.tensor_tensor(P1[:, 1], P1[:, 1], P2[:, 0], ALU.subtract))
                st.sync()
                first = P1[:, :, NPRE:T:DSEQ]
                st(ve.tensor_tensor(first, first, ah0[:, :, j, :], ALU.add))
                dve.wait_ge(dec_ready, j + 1)
                if j >= 2:
                    dve.wait_ge(rotated, 2 * (j - 1))
                st.sync()
                for r_ in range(2):
                    ve.tensor_tensor_scan(Gs[j % 2][:, r_], dec[j % 2], P1[:, r_], 0.0, ALU.mult, ALU.add)\
                      .then_inc(scanned, 1)

            def read_y(c):
                dve.wait_ge(h_used, 4 * (c + 1))
                ve.scalar_tensor_tensor(out=zT[:, c, :], in0=uT[:, c, N_META:T], scalar=dsk[:, c:c + 1],
                                        in1=ps[:, YB[c % 2], 0:TO], op0=ALU.mult, op1=ALU.add).then_inc(y_read, 1)

            dve.wait_ge(tables_ready, 1)
            tables(0)
            for j in range(NJ):
                if j % 4 == 2 and j < NJ - 4:
                    tables(j // 4 + 1)
                forward(j)
                if j % 4 == 2 and j >= 6:
                    read_y(j // 4 - 1)
            read_y(7)

            def flat(x):
                return x.rearrange("p c h i -> p (c h i)")
            dve.wait_ge(proj_read, TIDX[("gk", 3)] + 1)
            ve.memset(bG[:, 0, :, 0:PADT], 0.0).then_inc(gate_b, 1)
            dve.wait_ge(gate_abs, 3)
            dve.wait_ge(gate_b, 1)
            st(ve.scalar_tensor_tensor(out=flat(bG), in0=flat(bG), scalar=0.0, in1=flat(en), op0=ALU.min, op1=ALU.subtract))
            st.sync()
            st(ve.memset(bG[:, 0, :, 0:PADT], 0.0))
            st.sync()
            bf = flat(bG)
            npf = NCP * H * CL
            for i in range(3):
                st(ve.tensor_tensor_scan(bf[:, 384 * i:384 * i + 384], gmask32, bf[:, 384 * i:384 * i + 384], 0.0,
                                         ALU.mult, ALU.add))
            st(ve.tensor_tensor_scan(bf[:, npf:], gmask8, bf[:, npf:], 0.0, ALU.mult, ALU.add))
            st.sync()
            st(ve.tensor_scalar(flat(en), bf, -80.0 * 16, None, ALU.max))
            st.sync()
            dve.sem_inc(gate_b, 1)
            dve.sem_inc(gate_b, 1)
            dve.wait_ge(gate_exp, 1)
            dve.wait_ge(rotated, 2 * NJ)
            bp = bG[:, 0:NCP].rearrange("p c h i -> p (c h) i")
            bs = bG[:, NCP:].rearrange("p c h (s t) -> p (c h s) t", t=DSEQ)
            lastp, lasts = (glast[:, 0:36].unsqueeze(2), glast[:, 36:68].unsqueeze(2))
            st(ve.tensor_copy(lastp, bp[:, :, CL - 1:CL]))
            st(ve.tensor_copy(lasts, bs[:, :, DSEQ - 1:DSEQ]))
            st.sync()
            ve.tensor_tensor(bp, bc(lastp, 2, CL), bp, ALU.subtract).then_inc(gate_b, 1)
            ve.tensor_tensor(bs, bc(lasts, 2, DSEQ), bs, ALU.subtract).then_inc(gate_b, 1)
            ve.tensor_tensor(flat(qT), flat(qT), flat(eb), ALU.mult).then_inc(gates_ready, 1)
            dve.wait_ge(gate_exp, 3)
            ve.tensor_tensor(flat(en), flat(en), flat(kT), ALU.mult).then_inc(gates_ready, 1)
            dve.wait_ge(gates_ready, 2)
            ve.tensor_tensor(flat(kT), flat(kT), flat(bG), ALU.mult).then_inc(gates_ready, 1)

            def front(c):
                f = FB[c % 2]
                sample = c >= NCP
                n = H * SPC if sample else H
                dve.wait_ge(front_done, c + 1)
                if c == 0:
                    dve.wait_ge(hl_saved, NJ)
                if c >= 1:
                    dve.wait_ge(st_done, st_count(c))
                ve.tensor_tensor(PTm[c % 2], ps[:, f, 384:512], cmaskS if sample else cmaskP, ALU.mult)\
                  .then_inc(front_ready, 1)
                if sample:
                    qv = qT[:, c].unsqueeze(2)
                    for h_ in range(H):
                        st(ve.tensor_tensor(qexp[:, h_], bc(qT[:, c, h_:h_ + 1, :], 1, SPC), qmask, ALU.mult))
                    st.sync()
                ve.tensor_tensor(Kexp[:, 0:n], bc(ps[:, f, 256:384].unsqueeze(1), 1, n),
                                 bc((hsmask if sample else hmask).unsqueeze(2), 2, 128), ALU.mult)\
                  .then_inc(front_ready, 1)

            def add_states(c):
                n = 2 * SPC if c >= NCP else 2
                for i in range(n):
                    dve.wait_ge(st_done, st_count(c) + i + 1)
                    for x in range(2):
                        src = ps[:, 2 + i % 2, 256 * x:256 * x + 256]
                        if c < NCP:
                            h_ = 2 * i + x
                            dst, dcol = S[:, h_], eb[:, c, h_, CL - 1:CL]
                        else:
                            s_, h_ = i // 2, 2 * (i % 2) + x
                            dst = sstate[c - NCP][:, s_, h_]
                            dcol = eb[:, c, h_, DSEQ * s_ + DSEQ - 1:DSEQ * s_ + DSEQ]
                        if c == 0 and i == 0 and x == 0:
                            dve.wait_ge(masks_made, 3)
                        if x == 0 and c >= 1:
                            dve.wait_ge(st_added, 2 * st_count(c))
                        ve.scalar_tensor_tensor(out=dst, in0=dst, scalar=dcol, in1=src, op0=ALU.mult, op1=ALU.add)\
                          .then_inc(st_added, 1)

            def gate_s5(c):
                dve.wait_ge(proj_read, TIDX[("glu", c)] + 1)
                dve.wait_ge(z_ready, 1)
                ve.tensor_tensor(mixT[:, 8 + c, :], glu_t[c % 2], zT[:, c, :], ALU.mult).then_inc(mix_s5, 1)

            for c in range(NCH):
                front(c)
                add_states(c)
                p = GLA_TILE0 + c
                if p < len(TILES) and TILES[p][0] == "glu":
                    gate_s5(TILES[p][1])
            for p in range(GLA_TILE0 + NCH, len(TILES)):
                gate_s5(TILES[p][1])
            dve.wait_ge(o_read, NCH - 1)
            g10 = gss[:, 0:NCH - 1]
            ve.tensor_scalar(g10, g10, 1.0 / DV, EPS, ALU.mult, ALU.add).then_inc(o_sqrt, 1)
            dve.wait_ge(proj_read, TIDX[("r", 7)] + 1)
            st(ve.tensor_tensor(rT, rT, bc(ggla.unsqueeze(2), 2, TO), ALU.mult))
            dve.wait_ge(o_sqrt, 2)
            ve.reciprocal(gss[:, 16:16 + NCH - 1], g10).then_inc(o_rstd, 1)
            st.sync()
            for c in range(NCH - 1):
                for hf in range(2):
                    n = 2 * c + hf
                    dve.wait_ge(o_turned, n + 1)
                    dst = mixT[:, hf:8:2, CL * c:CL * c + CL]
                    ve.tensor_tensor(dst, ps[:, XB[n % 4], 0:128].rearrange("p (h i) -> p h i", i=CL),
                                     rT[:, hf:8:2, CL * c:CL * c + CL], ALU.mult).then_inc(mix_gla, 1)
            dve.wait_ge(res_loaded, 48)
            for i in range(8):
                for t in range(3):
                    dve.wait_ge(wout_done, 3 * i + t + 1)
                    d_ = hrow[0:TR[t], t, 256 * i:256 * i + 256]
                    ve.tensor_tensor(d_, d_, ps[0:TR[t], OB[i % 2][t], 0:256], ALU.add).then_inc(h_added, 1)
            dve.wait_ge(h_ss, 24)
            dve.wait_ge(rconst, 1)
            for t in range(3):
                st(ve.tensor_reduce(ssum[0:TR[t], t:t + 1], ssp[0:TR[t], t, :], AX.X, ALU.add))
            st.sync()
            ve.tensor_scalar(ssum[:, 0:3], ssum[:, 0:3], 1.0 / D, EPS, ALU.mult, ALU.add).then_inc(h_rstd, 1)
            dve.wait_ge(h_rstd, 2)
            st(ve.reciprocal(ssum[:, 4:7], ssum[:, 0:3]))
            st.sync()
            dve.wait_ge(ffn_loaded, 80)
            dve.wait_ge(wr_ready, 5)
            for t in range(3):
                rr = slice(0, TR[t])
                ve.scalar_tensor_tensor(out=hn[rr, t, :], in0=hrow[rr, t, :], scalar=ssum[rr, 4 + t:5 + t],
                                        in1=gffn[rr], op0=ALU.mult, op1=ALU.mult).then_inc(hn_ready, 1)
            dve.wait_ge(logits_done, 3)
            for t in range(3):
                rr = slice(0, TR[t])
                st(ve.tensor_tensor(Lg[rr, t, :], ps[rr, 4, 36 * t:36 * t + 36], br[rr], ALU.add))
            st.sync()
            st(ve.tensor_copy(lg8[:, :, 0:NG], Lg[:, :, 0:NG]))
            st.sync()
            for t in range(3):
                st(ve.max(gmx[:, t, :], lg8[:, t, :]))
            st.sync()
            for t in range(3):
                st(ve.max_index(gix[:, t, :], gmx[:, t, :], lg8[:, t, :]))
            ve.tensor_tensor(x4, Lg[:, :, 0:NG], bc(gmx[:, :, 0:1], 2, NG), ALU.subtract).then_inc(ex_in, 1)
            st.sync()
            st(ve.tensor_copy(gidx, gix[:, :, 0:1]))
            st.sync()
            st(ve.tensor_tensor(ohg, bc(iota32[:, 0:NG].unsqueeze(1), 1, 3), bc(gidx, 2, NG), ALU.is_equal))
            st.sync()
            for t in range(3):
                st(ve.tensor_tensor(lem[:, t], Lg[:, t, NG:].rearrange("p (g e) -> p g e", g=NG),
                                    bc(ohg[:, t, :].unsqueeze(2), 2, EPG), ALU.mult))
            st.sync()
            for t in range(3):
                st(ve.tensor_reduce(lsel[:, t, :], lem[:, t].rearrange("p g e -> p e g"), AX.X, ALU.add))
            st.sync()
            for t in range(3):
                st(ve.max(v8[:, t, :], lsel[:, t, :]))
            st.sync()
            for t in range(3):
                st(ve.max_index(ix8[:, t, :], v8[:, t, :], lsel[:, t, :]))
            ve.tensor_tensor(x1, v8[:, :, 1:2], v8[:, :, 0:1], ALU.subtract).then_inc(ex_in, 1)
            st.sync()
            st(ve.tensor_copy(eid, ix8[:, :, 0:2]))
            st(ve.tensor_scalar(gidx, gidx, float(EPG), None, ALU.mult))
            st.sync()
            st(ve.tensor_tensor(eid, eid, bc(gidx, 2, 2), ALU.add))
            st.sync()
            for k in range(2):
                st(ve.tensor_tensor(M[:, :, k, :], bc(iota32.unsqueeze(1), 1, 3), bc(eid[:, :, k:k + 1], 2, NE), ALU.is_equal))
            st.sync()
            st(ve.memset(M[NS:, 2], 0.0))
            st.sync()
            ve.tensor_tensor(M01, M[:, :, 0, :], M[:, :, 1, :], ALU.add).then_inc(m_ready, 1)
            dve.wait_ge(ex_out, 2)
            st(ve.tensor_reduce(u1[0], x4, AX.X, ALU.add))
            st(ve.tensor_scalar(u1[1], x1, 1.0, None, ALU.add))
            st.sync()
            st(ve.tensor_tensor(u1[2], u1[0], u1[1], ALU.mult))
            st.sync()
            st(ve.reciprocal(ewt[:, :, 0:1], u1[2]))
            st.sync()
            st(ve.tensor_tensor(ewt[:, :, 1:2], ewt[:, :, 0:1], x1, ALU.mult))
            dve.wait_ge(rank_done, 1)
            st(ve.tensor_copy(cnt, ps[:, 4, 3 * NE:4 * NE]))
            st.sync()
            st(ve.tensor_scalar(ov, cnt, CAP + 0.5, None, ALU.is_ge))
            for m in range(2, TO // CAP):
                st(ve.tensor_scalar(t32[(m - 2) % 2], cnt, CAP * m + 0.5, None, ALU.is_ge))
                st.sync()
                st(ve.tensor_tensor(ov, ov, t32[(m - 2) % 2], ALU.add))
            st.sync()
            st(ve.tensor_tensor_scan(ovc, ones[:, 0:NE], ov, 0.0, ALU.mult, ALU.add))
            for t in range(3):
                st(ve.tensor_tensor(Mx[:, t], M[:, t], bc(ps[:, 4, NE * t:NE * t + NE].unsqueeze(1), 1, 2), ALU.mult))
            st.sync()
            st(ve.tensor_tensor(ov, ovc, ov, ALU.subtract))
            st(ve.tensor_reduce(u2[0], Mx, AX.X, ALU.add))
            st.sync()
            for t in range(3):
                st(ve.tensor_tensor(Mx[:, t], M[:, t], bc(ov.unsqueeze(1), 1, 2), ALU.mult))
            st(ve.tensor_scalar(u2[2], u2[0], CAP - 0.5, None, ALU.is_ge))
            st.sync()
            st(ve.tensor_reduce(u2[1], Mx, AX.X, ALU.add))
            st(ve.scalar_tensor_tensor(out=u2[3], in0=eid, scalar=float(CAP), in1=u2[0], op0=ALU.mult, op1=ALU.add))
            st.sync()
            st(ve.tensor_tensor(u2[1], u2[1], eid, ALU.subtract))
            st.sync()
            st(ve.tensor_scalar(u2[1], u2[1], float(NE - 1), float(CAP), ALU.add, ALU.mult))
            st.sync()
            st(ve.tensor_tensor(u2[1], u2[1], u2[2], ALU.mult))
            st.sync()
            st(ve.tensor_tensor(u2[3], u2[3], u2[1], ALU.add))
            st.sync()
            ve.tensor_copy(dest, u2[3]).then_inc(dest_ready, 1)
            st(ve.tensor_tensor(cmp9[0:1], bc(ovc[0:1, :].unsqueeze(1), 1, NOVF),
                                bc(iota32[0:1, 0:NOVF].unsqueeze(2), 2, NE), ALU.is_le))
            st.sync()
            st(ve.tensor_reduce(f9[0:1], cmp9[0:1], AX.X, ALU.add))
            st.sync()
            st(ve.tensor_scalar(f9[0:1], f9[0:1], float(NE - 1), None, ALU.min))
            st.sync()
            st(ve.tensor_copy(ovexp[0:1], f9[0:1]))
            st(ve.tensor_copy(novf[0:1], ovc[0:1, NE - 1:NE]))
            st.sync()
            for _ in range(1):
                dve.sem_inc(small_done, 1)

            def expert(n, first=False):
                dve.wait_ge(x_turned, 2 * n + 2)
                ve.tensor_copy(xT[:, 8:16].rearrange("p k t -> p (k t)"), ps[:, 3, :]).then_inc(xT_b, 1)
                dve.wait_ge(weights_used, 12 * n + 8)
                ve.tensor_copy(GUs, ps[:, 0, :]).then_inc(gu_copied, 1)
                dve.wait_ge(silu_ready, n + 1)
                gt = ps[:, 1, :].rearrange("p (k x t) -> p k x t", k=4, x=2)
                ve.tensor_tensor(HT, Hs, gt[:, :, 1, :], ALU.mult).then_inc(hid_ready, 1)
                dve.wait_ge(weights_used, 12 * (n + 1))
                if not first:
                    dve.wait_ge(stored, 32 * n)
                ve.tensor_copy(Os[:, 1, :], ps[:, 7, :]).then_inc(out_b, 1)

            expert(0, True)
            with dve.Fori(1, NE) as e:
                expert(e)
            n_over = dve.value_load(novf[0:1, 0:1], min_val=0, max_val=NOVF)
            with dve.Fori(0, NOVF) as o:
                with dve.If(n_over > o):
                    expert(o + NE)
                dve.nop()
            dve.wait_ge(gfin_loaded, 16)
            for t in range(3):
                rr = slice(0, TR[t])
                dve.wait_ge(gathered[t], 32)
                fs = Steps(dve, fin_chain[t])
                fs(ve.scalar_tensor_tensor(out=hrow[rr, t, :], in0=yrows[2 * t][rr], scalar=ewt[rr, t, 0:1],
                                           in1=hrow[rr, t, :], op0=ALU.mult, op1=ALU.add))
                fs.sync()
                ve.scalar_tensor_tensor(out=hrow[rr, t, :], in0=yrows[2 * t + 1][rr], scalar=ewt[rr, t, 1:2],
                                        in1=hrow[rr, t, :], op0=ALU.mult, op1=ALU.add).then_inc(fin_ss, 1)
                x_ = ssum[rr, 8 + t:9 + t]
                dve.wait_ge(fin_rstd, 2 * t + 1)
                ve.tensor_scalar(x_, x_, 1.0 / D, EPS, ALU.mult, ALU.add).then_inc(fin_ss, 1)
                dve.wait_ge(fin_rstd, 2 * t + 2)
                fs(ve.reciprocal(ssum[rr, 12 + t:13 + t], x_))
                fs.sync()
                ve.scalar_tensor_tensor(out=hn[rr, t, :], in0=hrow[rr, t, :], scalar=ssum[rr, 12 + t:13 + t],
                                        in1=gfin[rr], op0=ALU.mult, op1=ALU.mult).then_inc(fin_ready, 1)

        @block.tensor
        def _(pe):
            te = nc.tensor
            pe.wait_ge(ident_made, 1)
            for n in range(12):
                t, g = n // 4, n % 4
                pe.wait_ge(xn_scaled, t + 1)
                if n >= 4:
                    pe.wait_ge(xn_ready, n - 3)
                for k in range(4):
                    mm = te.transpose(ps[:, XB[n % 4], XT_ROWS * k:XT_ROWS * k + XT_ROWS],
                                      xr[:, t, 4 * g + k:D:KT], ident[0:XT_ROWS, 0:XT_ROWS])
                mm.then_inc(xn_turned, 1)
                if n == 3:
                    pe.wait_ge(s5_loaded, 128)
                    for r_ in range(2):
                        mm = te.transpose(ps[:, 4, NJ * r_:NJ * r_ + NJ], lam_ld[:, r_, :], ident[0:NJ, 0:NJ])
                    mm.then_inc(prm_turned, 1)
                    for m in range(4):
                        mm = te.transpose(ps[:, 7, 128 * m:128 * m + 128], st_ld[:, m, :], ident)
                    mm.then_inc(prm_turned, 1)
            pe.wait_ge(xn_ready, 12)

            def turn_pad(k):
                pe.wait_ge(pad_ready, k + 1)
                if k == 1:
                    pe.wait_ge(bt_ready, 4)
                for i in range(4):
                    if k == 1 and i >= 2:
                        pe.wait_ge(ct_ready, i - 1)
                    for x in range(4):
                        mm = te.transpose(ps[:, TB[k][i], 128 * x:128 * x + 128], pad[:, i // 2, 4 * (i % 2) + x, :], ident)
                    mm.then_inc(pad_turned, 1)

            def s5_in(j):
                c, q = j // 4, j % 4
                rows = slice(32 * q, 32 * q + 32)
                pe.wait_ge(proj_read, c + 1)
                if j == 0:
                    pe.wait_ge(bt_ready, 4)
                if j >= 2:
                    pe.wait_ge(bu_read, j - 1)
                for r_ in range(2):
                    te.matmul(ps[:, BU[j % 2][r_], 0:T], BT[rows, r_, c, :], uT[rows, c, :], start=True, stop=True)\
                      .then_inc(bu_done, 1)

            def s5_out(j):
                c, q = j // 4, j % 4
                cols_ = slice(32 * q, 32 * q + 32)
                pe.wait_ge(rotated, 2 * (j + 1))
                if j == 0:
                    pe.wait_ge(ct_ready, 4)
                if q == 0 and c >= 2:
                    pe.wait_ge(y_read, c - 1)
                for r_ in range(2):
                    mm = te.matmul(ps[cols_, YB[c % 2], 0:TO], CT[:, r_, c, cols_], Q1[j % 2][:, r_, N_META:T],
                                   start=(r_ == 0), stop=(r_ == 1))
                mm.then_inc(h_used, 1)

            def gla_front(c):
                f = FB[c % 2]
                if c == 0:
                    pe.wait_ge(gates_ready, 3)
                    pe.wait_ge(y_read, 8)
                    pe.wait_ge(masks_made, 2)
                if c >= 1:
                    pe.wait_ge(v_copied, c)
                if c >= 2:
                    pe.wait_ge(front_ready, 2 * (c - 1))
                for hf in range(2):
                    te.transpose(ps[:, 4, 128 * hf:128 * hf + 128], vT[:, hf, c, :], ident)
                te.transpose(ps[:, f, 256:384], chunk_view(kT[:, c]), ident)
                te.matmul(ps[:, f, 384:512], chunk_view(en[:, c]), chunk_view(qT[:, c]), start=True, stop=True)\
                  .then_inc(front_done, 1)

            def gla_back(c):
                sample = c >= NCP
                pe.wait_ge(v_copied, c + 1)
                pe.wait_ge(front_ready, 2 * (c + 1))
                if c >= 2:
                    pe.wait_ge(o_read, c - 1)
                if c >= 1:
                    pe.wait_ge(st_added, 2 * st_count(c))
                if sample:
                    pe.wait_ge(ss_loaded[c - NCP], 16 * SPC)
                if c:
                    te.matmul(ps[:, 6, 0:DV], PTm[c % 2], Vn[c % 2], start=True, stop=False, skip_group_check=True)
                    for s_ in range(SPC if sample else 1):
                        for h_ in range(H):
                            rows = slice(CL * h_, CL * h_ + CL)
                            lhs = qexp[:, h_, s_, :] if sample else qT[:, c, h_, :]
                            rhs = sstate[c - NCP][:, s_, h_] if sample else S[:, h_]
                            last = s_ == (SPC if sample else 1) - 1
                            mm = te.matmul(ps[rows, 6, 0:DV], lhs, rhs, start=False, stop=last, skip_group_check=True)
                    mm.then_inc(o_done, 1)
                n = 2 * SPC if sample else 2
                for i in range(n):
                    if i >= 2:
                        pe.wait_ge(st_added, 2 * (st_count(c) + i - 1))
                    for x in range(2):
                        if sample:
                            m = (2 * (i % 2) + x) * SPC + i // 2
                        else:
                            m = 2 * i + x
                        mm = te.matmul(ps[:, 2 + i % 2, 256 * x:256 * x + 256], Kexp[:, m, :], Vn[c % 2],
                                       start=True, stop=True)
                    mm.then_inc(st_done, 1)

            slot = 0
            for p, (kind, i) in enumerate(TILES):
                if p == 2:
                    turn_pad(0)
                if p == 4:
                    turn_pad(1)
                c = p - GLA_TILE0
                if 0 <= c < NCH:
                    gla_front(c)
                if p >= 2:
                    pe.wait_ge(proj_read, p - 1)
                n = CIDX[(kind, i // 2)] if kind in ("u", "q", "k", "v", "r", "glu") else None
                if n is not None and i % 2 == 0:
                    pe.wait_ge(ring_loaded[n % 2], 16 * (n // 2 + 1))
                if kind == "glu" and i == 0:
                    pe.wait_ge(z_ready, 1)
                if kind in ("a", "gk"):
                    pe.wait_ge(small_loaded, 7 * 16)
                kt = 8 if kind == "glu" else 1 if kind == "gk" else KT
                if kind == "gk":
                    pe.wait_ge(proj_read, TIDX[("a", 0)] + 1)
                for k in range(kt):
                    if k == (kt // 2 if kt > 1 else 0):
                        for j in bu_at[2 * p + 1]:
                            s5_in(j)
                        for j in y_at[2 * p + 1]:
                            s5_out(j)
                        if 0 <= c < NCH:
                            gla_back(c)
                    if k == 0:
                        for j in bu_at[2 * p]:
                            s5_in(j)
                        for j in y_at[2 * p]:
                            s5_out(j)
                    out = ps[:, p % 2, 0:T]
                    if kind == "a":
                        mm = te.matmul(ps[0:RANK, p % 2, 0:T], wa[:, k, :], xnT[:, k, :], start=(k == 0), stop=(k == kt - 1))
                    elif kind == "gk":
                        mm = te.matmul(out, wgk[:, DK * i:DK * i + DK], aT, start=True, stop=True)
                    else:
                        w = ring[n % 2][:, 0:256 * kt].rearrange("p (k n) -> p k n", n=256)[:, k, 128 * (i % 2):128 * (i % 2) + 128]
                        x = zT[:, k, :] if kind == "glu" else xnT[:, k, N_META:T] if kind == "r" else xnT[:, k, :]
                        o = out if kind not in ("r", "glu") else out[:, 0:TO]
                        mm = te.matmul(o, w, x, start=(k == 0), stop=(k == kt - 1))
                mm.then_inc(proj_done, 1)
            for c in range(len(TILES) - GLA_TILE0, NCH):
                gla_front(c)
                gla_back(c)
            pe.wait_ge(hl_saved, NJ)
            pe.wait_ge(st_added, 2 * st_count(NCH))
            for r_ in range(2):
                te.transpose(ps[0:NJ, 2 + r_, 0:128], hl[:, r_, 0, :], ident)
                for m in range(2):
                    mm = te.transpose(ps[:, 2 + r_, 128 + 128 * m:256 + 128 * m],
                                      hl[:, r_, 1 + 4 * m:5 + 4 * m, :].rearrange("p s j -> p (s j)"), ident)
                mm.then_inc(hl_turned, 1)
            pe.wait_ge(hl_copied, 2)
            for c in range(NCH - 1):
                pe.wait_ge(o_scaled, c + 1)
                for hf in range(2):
                    n = 2 * c + hf
                    if n >= 4:
                        pe.wait_ge(mix_gla, n - 3)
                    te.transpose(ps[:, XB[n % 4], 0:128], o_all[:, c, 128 * hf:128 * hf + 128], ident).then_inc(o_turned, 1)
            pe.wait_ge(mix_s5, 8)
            pe.wait_ge(mix_gla, 2 * (NCH - 1))
            for i in range(8):
                n = CIDX[("out", i)]
                pe.wait_ge(ring_loaded[n % 2], 16 * (n // 2 + 1))
                w = ring[n % 2].rearrange("p (k n) -> p k n", n=256)
                for t in range(3):
                    if i >= 2:
                        pe.wait_ge(h_added, 3 * (i - 2) + t + 1)
                    for m in range(16):
                        mm = te.matmul(ps[0:TR[t], OB[i % 2][t], 0:256], mixT[:, m, 128 * t:128 * t + TR[t]], w[:, m, :],
                                       start=(m == 0), stop=(m == 15))
                    mm.then_inc(wout_done, 1)
            pe.wait_ge(h_added, 24)
            for n in range(12):
                t, g_ = n // 4, n % 4
                pe.wait_ge(hn_ready, t + 1)
                if n >= 4:
                    pe.wait_ge(hnT_ready, n - 3)
                for k in range(4):
                    mm = te.transpose(ps[:, XB[n % 4], TR[t] * k:TR[t] * k + TR[t]], hn[0:TR[t], t, 4 * g_ + k:D:KT],
                                      ident[0:TR[t], 0:TR[t]])
                mm.then_inc(hn_turned, 1)
            pe.wait_ge(hnT_ready, 12)
            for t in range(3):
                for k in range(KT):
                    mm = te.matmul(ps[0:TR[t], 4, 36 * t:36 * t + 36], hnT[:, k, 128 * t:128 * t + TR[t]], Wr[:, k, :],
                                   start=(k == 0), stop=(k == KT - 1))
                mm.then_inc(logits_done, 1)
            pe.wait_ge(m_ready, 1)
            for t in range(4):
                for t2 in range(min(t + 1, 3)):
                    mm = te.matmul(ps[:, 4, NE * t:NE * t + NE], tri if t2 == t else ones, M01[:, t2, :],
                                   start=(t2 == 0), stop=(t2 == min(t, 2)))
            mm.then_inc(rank_done, 1)

            def expert(n, first=False):
                pe.wait_ge(xrow_loaded, 16 * (n + 1))
                for b in range(2):
                    for k in range(8):
                        turn = te.matmul if b + k == 0 else te.transpose
                        mm = turn(ps[:, 2 + b, CAP * k:CAP * k + CAP], xrow[:, 8 * b + k:D:KT], ident[0:CAP, 0:CAP])
                    mm.then_inc(x_turned, 1)
                pe.wait_ge(xT_a, n + 1)
                pe.wait_ge(xT_b, n + 1)
                for q in range(4):
                    pe.wait_ge(piece_loaded[2 * q], 16 * (n + 1))
                    pe.wait_ge(piece_loaded[2 * q + 1], 16 * (n + 1))
                    for k in range(4):
                        for x in range(2):
                            mm = te.matmul(ps[CAP * x:CAP * x + CAP, 0, :], xT[:, 4 * q + k, :],
                                           wpiece[2 * q + x][:, HID * k:HID * k + HID],
                                           start=(q == 0 and k == 0), stop=(q == 3 and k == 3))
                    mm.then_inc(weights_used, 2)
                pe.wait_ge(gu_copied, n + 1)
                for k in range(4):
                    mm = te.transpose(ps[:, 1, 128 * k:128 * k + 128], GUs[:, k:HID:4], ident)
                mm.then_inc(gu_turned, 1)
                pe.wait_ge(hid_ready, n + 1)
                if not first:
                    pe.wait_ge(out_a, n)
                    pe.wait_ge(out_b, n)
                for k in range(4):
                    pe.wait_ge(piece_loaded[8 + k], 16 * (n + 1))
                    for j in range(2):
                        for x in range(2):
                            mm = te.matmul(ps[CAP * x:CAP * x + CAP, 6 + j, :], HT[:, k, :],
                                           wpiece[8 + k][:, 512 * (2 * j + x):512 * (2 * j + x) + 512],
                                           start=(k == 0), stop=(k == 3))
                    mm.then_inc(weights_used, 1)

            expert(0, True)
            with pe.Fori(1, NE) as e:
                expert(e)
            pe.wait_ge(small_done, 1)
            n_over = pe.value_load(novf[0:1, 0:1], min_val=0, max_val=NOVF)
            with pe.Fori(0, NOVF) as o:
                with pe.If(n_over > o):
                    expert(o + NE)
                pe.nop()


_INS = ["x_prompt", "x_sample", "state_gla", "state_s5_re", "state_s5_im", "meta", "g_mix", "w_in", "w_gk2", "b_gk",
        "g_gla", "lam_re", "lam_im", "log_dt", "s5_b_re", "s5_b_im", "s5_c_re", "s5_c_im", "d_skip", "w_glu", "b_glu",
        "w_out", "g_ffn", "w_rg", "b_rg", "w_re", "b_re", "w_gate", "w_up", "w_down", "g_final"]
_OUTS = {"y_prompt": (1, 256, 2048), "y_sample": (8, 8, 2048), "new_gla_prompt": (1, 1, 4, 128, 256),
         "new_s5_re_prompt": (1, 1, 64, 64), "new_s5_im_prompt": (1, 1, 64, 64), "new_gla_sample": (1, 8, 4, 128, 256),
         "new_s5_re_sample": (1, 8, 64, 64), "new_s5_im_sample": (1, 8, 64, 64)}


def kernel(**inputs):
    import numpy as _np
    import concourse.bacc as _bacc
    from concourse import mybir as _mybir
    from concourse.bass_utils import run_bass_kernel_spmd as _run

    nc = _bacc.Bacc("TRN2", target_bir_lowering=False, num_devices=1)
    arrays, args = {}, {}
    for name in _INS:
        a = _np.ascontiguousarray(inputs[name])
        arrays[f"in_{name}"] = a
        args[name] = nc.dram_tensor(f"in_{name}", a.shape, _mybir.dt.from_np(a.dtype), kind="ExternalInput").ap()
    for name, shape in _OUTS.items():
        args[name] = nc.dram_tensor(f"out_{name}", shape, _mybir.dt.float32, kind="ExternalOutput").ap()
    build(nc, args)
    r = _run(nc, [arrays], core_ids=[0])
    return tuple(r.results[0][f"out_{name}"] for name in _OUTS)
```

```python
import math
from contextlib import ExitStack

import concourse.bass as bass
from concourse import mybir

F32 = mybir.dt.float32
I32 = mybir.dt.int32
U32 = mybir.dt.uint32
BF16 = mybir.dt.bfloat16
ALU = mybir.AluOpType
ACT = mybir.ActivationFunctionType
AX = mybir.AxisListType

D = 2048
KT = D // 128
N_META, SEQ, NSEQ, DSEQ = 16, 256, 8, 8
NPRE = N_META + SEQ
NS = NSEQ * DSEQ
T = NPRE + NS
TO = SEQ + NS
XT_ROWS = T // 3
H, DK, DV = 4, 128, 256
RANK = 16
G, P, GC = 64, 64, 16
NJ = G * P // 128
CL = 32
NCP = (NPRE + CL - 1) // CL
PADT = NCP * CL - NPRE
NCS = NS // CL
NCH = NCP + NCS
SPC = CL // DSEQ
NG, EPG, NE, HID = 4, 8, 32, 512
CAP = 64
NA = 2 * TO
NOVF = (NA - 1) // (CAP + 1)
NPAIR = NE // 2
NL = NG + NE
NOP = (NOVF + 1) // 2
EPS = 1e-6
OFF_Q, OFF_K, OFF_V, OFF_R, OFF_A, OFF_U = 0, 512, 1024, 2048, 3072, 3088
MAGIC = 1.5 * 2.0 ** 23
TWO_PI_1 = 6.28125
TWO_PI_2 = 0.0019350051879882812
TWO_PI_3 = 2.0 * math.pi - TWO_PI_1 - TWO_PI_2
BIG = 3.0e38
ARENA = 53188

TILES = ([("u", c) for c in range(8)] + [("a", 0)] + [("q", h) for h in range(4)] + [("k", h) for h in range(4)]
         + [("v", m) for m in range(8)] + [("gk", h) for h in range(4)] + [("r", m) for m in range(8)]
         + [("glu", c) for c in range(8)])
TIDX = {t: i for i, t in enumerate(TILES)}
CHUNKS = ([("u", i) for i in range(4)] + [("q", i) for i in range(2)] + [("k", i) for i in range(2)]
          + [("v", i) for i in range(4)] + [("r", i) for i in range(4)] + [("glu", i) for i in range(4)]
          + [("out", i) for i in range(8)])
CIDX = {c: i for i, c in enumerate(CHUNKS)}
COL0 = {"u": OFF_U, "q": OFF_Q, "k": OFF_K, "v": OFF_V, "r": OFF_R}
GLA_TILE0 = TIDX[("r", 2)]


PAD_B_TILE, PAD_C_TILE = 3, 6


def s5_half_steps():
    return [2 * PAD_C_TILE - 1 + (j * 17) // 16 for j in range(NJ)]


class Steps:

    def __init__(self, eng, sem):
        self.eng, self.sem, self.n = eng, sem, 0

    def __call__(self, ins):
        ins.then_inc(self.sem, 1)
        self.n += 1

    def sync(self):
        if self.n:
            self.eng.wait_ge(self.sem, self.n)


class Region:
    def __init__(self, arena, start, size):
        self.arena, self.at, self.end = arena, start, start + size

    def take(self, *shape, parts=128):
        n = int(math.prod(shape))
        a = self.arena[0:parts, self.at:self.at + n]
        self.at += n
        assert self.at <= self.end, (self.at, self.end)
        if len(shape) == 1:
            return a
        names = "abcd"[:len(shape)]
        return a.rearrange(f"p ({' '.join(names)}) -> p {' '.join(names)}", **dict(zip(names[1:], shape[1:])))


def bc(ap, axis, n):
    shape = list(ap.shape)
    assert shape[axis] == 1
    shape[axis] = n
    return ap.broadcast_to(shape)


def build(nc, A):
    ctx = ExitStack()
    with ctx:
        def sem(name):
            return ctx.enter_context(nc.semaphore(name))

        arena = ctx.enter_context(nc.sbuf_tensor("arena", [128, ARENA], F32))
        ps = ctx.enter_context(nc.psum_tensor("ps", [128, 8, 512], F32))

        SIZE_A, SIZE_B, SIZE_C, SIZE_D = 24576, 8192, 5120, 12288
        at_b = SIZE_A
        at_c = at_b + SIZE_B
        at_d = at_c + SIZE_C
        at_x = at_d + SIZE_D
        ra = Region(arena, 0, SIZE_A)
        E = ra.take(2, 2, 4 * T)
        E = [E[:, b].rearrange("p r (j t) -> p r j t", j=4) for b in range(2)]
        at_xn = ra.at
        xnT = ra.take(KT, T)
        at_u = ra.at
        uT = ra.take(8, T)
        qT = ra.take(NCH, H, CL)
        kT = ra.take(NCH, H, CL)
        at_v = ra.at
        vT = ra.take(2, NCH, H * CL)
        rT = ra.take(8, TO)
        aT = ra.take(T, parts=RANK)
        at_g = ra.at
        bG = ra.take(NCH, H, CL)
        wgk = ra.take(H * DK, parts=RANK)
        wa = ra.take(KT, RANK)
        gmask32 = ra.take(384)
        glu_t = [Region(arena, ra.at - 384, 384).take(TO), Region(arena, at_g - T, T).take(TO)]
        xr = arena[0:XT_ROWS, at_v:at_v + 3 * D].rearrange("p (t d) -> p t d", t=3)
        r = Region(arena, at_g, NCH * H * CL)
        h0 = r.take(2, NSEQ, NJ)
        ah0 = r.take(2, NJ, NSEQ)
        r = Region(arena, 0, at_xn)
        sstate = [r.take(SPC, H, DV), Region(arena, at_xn, 4096).take(SPC, H, DV)]
        qexp = r.take(H, SPC, CL)
        junk = r.take(DV)
        PTm = [r.take(128) for _ in range(2)]
        gss = r.take(32)
        glast = r.take(68)
        o_all = Region(arena, at_u, 2688).take(NCH - 1, DV)
        r = Region(arena, 0, SIZE_A)
        wpiece = [r.take(2048) for _ in range(12)]
        ring = [arena[:, at_b + 4096 * i:at_b + 4096 * (i + 1)] for i in range(2)]
        r = Region(arena, at_b, SIZE_B)
        Psel = r.take(3, 2 * CAP)
        slot = r.take(2 * CAP)
        destf = r.take(3, 2)
        r = Region(arena, at_b + D, SIZE_B - D)
        xT = r.take(KT, 2 * CAP)
        GUs = r.take(HID)
        Hs = r.take(4, CAP)
        HT = r.take(4, CAP)
        rt = Region(arena, at_b + SIZE_B - 1024, 1024)
        mixT = Region(arena, at_c, SIZE_C).take(16, TO)
        hnT = Region(arena, at_c, SIZE_C).take(KT, TO)
        r = Region(arena, at_c, SIZE_C)
        Os = r.take(D)
        slotB, ewtB = r.take(2, TO), r.take(2, TO)
        Wh, Wsel = r.take(2, TO), r.take(TO)
        diag = Region(arena, at_c, D).take(3, 4, 128)
        r = Region(arena, at_c, 8 * TO)
        lam_ld = r.take(2, 128, parts=NJ)
        st_ld = r.take(4, 128)
        b_ld = r.take(2, NJ * GC)
        prm = r.take(21, NJ)
        r = Region(arena, at_c + 8 * TO, 8 * TO)
        Bt = r.take(2, NJ, 16)
        At = r.take(2, NJ, 17)
        r = Region(arena, at_d, SIZE_D)
        eb = r.take(NCH, H, CL)
        en = r.take(NCH, H, CL)
        at_z = r.at
        zT = r.take(8, TO)
        at_S = r.at
        S = r.take(H, DV)
        BT = r.take(2, 8, 128)
        CT = r.take(2, 8, 128)
        at_m = r.at
        hl = r.take(2, 9, NJ)
        cmaskS = r.take(128)
        qmask = r.take(SPC, CL)
        s5mask = r.take(T)
        gmask8 = r.take(256)
        pad = Region(arena, at_z, 2560).take(2, 8, 128)
        c_ld = Region(arena, at_S, 1024).take(2, 8, P)
        r = Region(arena, at_d, 2816)
        P1, P2 = r.take(2, T), r.take(2, T)
        Gs = [r.take(2, T), r.take(2, T)]
        ets = Region(arena, at_d, 1344).take(4, 17, 16)
        hrow = Region(arena, at_d, 6144).take(3, D)
        hn = Region(arena, at_d + 6144, 6144).take(3, D)
        r = Region(arena, at_x, ARENA - at_x)
        ident = r.take(128)
        cmaskP = r.take(128)
        hmask = r.take(H)
        hsmask = r.take(H * SPC)
        gmix = r.take(KT)
        warm = r.take(1, parts=1)
        ggla, dsk, bgk, bglu = r.take(8), r.take(8), r.take(H), r.take(8)
        at_x2 = r.at
        Q1 = [r.take(2, T), r.take(2, T)]
        Q2 = r.take(2, T)
        dec = [r.take(T), r.take(T)]
        r = Region(arena, at_x2, 2688)
        Kexp = r.take(H * SPC, 128)
        Vn = [r.take(DV) for _ in range(2)]
        gffn = Region(arena, at_x2, 2688).take(D)
        gfin = Region(arena, at_x2, 2688).take(D)
        hlT = Region(arena, at_x2, 2688).take(6, 128)
        r = Region(arena, at_x2 + D, 640)
        Wr = r.take(KT, NG + NE)
        br = r.take(NG + NE)
        ssp = r.take(3, 8)
        wrg_ld = Region(arena, at_d + 6144, 64).take(KT, NG)
        wre_ld = Region(arena, at_d + 6208, 512).take(NG, KT, EPG)
        r = rt
        ewt = r.take(3, 2)
        slotp = r.take(1)
        slotpi = r.take(1).bitcast(I32)
        ovexp = r.take(2 * NOP).bitcast(I32)
        novf = r.take(1).bitcast(I32)
        ssum = r.take(16)
        tri, ones = r.take(128), r.take(128)
        iota32 = r.take(NE)
        iota32i = r.take(NE).bitcast(I32)
        sloti = r.take(2 * CAP).bitcast(I32)
        r = Region(arena, at_b + D + KT * 2 * CAP, 2048)
        Lg = r.take(3, NG + NE)
        lg8, gmx, gix, gidx = r.take(3, 8), r.take(3, 8), r.take(3, 8).bitcast(U32), r.take(3, 1)
        ohg, lem, lsel = r.take(3, NG), r.take(3, NG, EPG), r.take(3, 8)
        v8, ix8, eid = r.take(3, 8), r.take(3, 8).bitcast(U32), r.take(3, 2)
        M, Mx = r.take(3, 2, NE), r.take(3, 2, NE)
        M01 = r.take(3 * NE // 2).bitcast(BF16).rearrange("p (t e) -> p t e", t=3)
        tri16, ones16 = r.take(64).bitcast(BF16), r.take(64).bitcast(BF16)
        x4, x1 = r.take(3, NG), r.take(3, 1)
        u2 = [r.take(3, 2) for _ in range(6)]
        u1 = [r.take(3, 1) for _ in range(6)]
        cnt, ov, ovc, t32 = r.take(NE), r.take(NE), r.take(NE), [r.take(NE), r.take(NE)]
        novb = r.take(NE)
        logT = Region(arena, at_b + D, 2 * TO).take(2, TO, parts=NL)
        ovcmp = r.take(2 * NOP, NE)
        ovf = r.take(2 * NOP)
        hjunk = Region(arena, at_d + 6144 + 1024, 256).take(256)
        xss = Region(arena, at_g + 1024, 16).take(2, 3)

        x_loaded = [sem(f"x_loaded{t}") for t in range(3)]
        ring_loaded = [sem("ring_loaded0"), sem("ring_loaded1")]
        xn_sq, xn_mean = sem("xn_sq"), sem("xn_mean")
        xn_sqrt, xn_rstd = sem("xn_sqrt"), sem("xn_rstd")
        s_stored, states_stored = sem("s_stored"), sem("states_stored")
        gmix_loaded = sem("gmix_loaded")
        small_loaded = sem("small_loaded")
        s5_loaded = sem("s5_loaded")
        ldt_loaded = sem("ldt_loaded")
        c_loaded = sem("c_loaded")
        masks_made = sem("masks_made")
        ident_made = sem("ident_made")
        pool_steps, act_steps, dve_steps = sem("pool_steps"), sem("act_steps"), sem("dve_steps")
        xn_scaled = [sem(f"xn_scaled{t}") for t in range(3)]
        lam_loaded = sem("lam_loaded")
        xn_turned = sem("xn_turned")
        xn_ready = sem("xn_ready")
        prm_turned = sem("prm_turned")
        prm_ready = sem("prm_ready")
        h0_ready = sem("h0_ready")
        dt_ready = sem("dt_ready")
        arg_ready = sem("arg_ready")
        trig_ready = sem("trig_ready")
        tables_ready = sem("tables_ready")
        pad_ready = sem("pad_ready")
        pad_turned = sem("pad_turned")
        bt_ready, ct_ready = sem("bt_ready"), sem("ct_ready")
        proj_done = sem("proj_done")
        proj_read = sem("proj_read")
        bu_done = sem("bu_done")
        bu_read = sem("bu_read")
        dec_ready = sem("dec_ready")
        scanned = sem("scanned")
        rotated = sem("rotated")
        h_used = sem("h_used")
        hl_saved = sem("hl_saved")
        y_read = sem("y_read")
        z_ready = sem("z_ready")
        gate_abs = sem("gate_abs")
        gate_b = sem("gate_b")
        gate_exp = sem("gate_exp")
        gates_ready = sem("gates_ready")
        ss_loaded = [sem("ss_loaded0"), sem("ss_loaded1")]
        front_done = sem("front_done")
        v_copied = sem("v_copied")
        front_ready = sem("front_ready")
        o_done = sem("o_done")
        o_read = sem("o_read")
        st_done = sem("st_done")
        st_added = sem("st_added")
        o_sqrt = sem("o_sqrt")
        o_rstd = sem("o_rstd")
        o_scaled = sem("o_scaled")
        o_turned = sem("o_turned")
        mix_gla = sem("mix_gla")
        mix_s5 = sem("mix_s5")
        stores = sem("stores")
        y_stored = sem("y_stored")
        hl_turned = sem("hl_turned")
        hl_copied = sem("hl_copied")
        res_loaded = sem("res_loaded")
        wout_done = sem("wout_done")
        h_added = sem("h_added")
        ffn_loaded = sem("ffn_loaded")
        wr_ready = sem("wr_ready")
        h_ss = sem("h_ss")
        h_rstd = sem("h_rstd")
        hn_ready = sem("hn_ready")
        hn_turned = sem("hn_turned")
        hnT_ready = sem("hnT_ready")
        logits_done = sem("logits_done")
        logitsT_ready = sem("logitsT_ready")
        logits_turned = sem("logits_turned")
        rconst = sem("rconst")
        ex_in, ex_out = sem("ex_in"), sem("ex_out")
        m_ready = sem("m_ready")
        rank_done = sem("rank_done")
        dest_ready = sem("dest_ready")
        piece_loaded = [sem(f"piece_loaded{i}") for i in range(12)]
        weights_used = sem("weights_used")
        p_step, p_half = sem("p_step"), sem("p_half")
        p_ready = sem("p_ready")
        x_turned = sem("x_turned")
        xT_a, xT_b = sem("xT_a"), sem("xT_b")
        gu_copied = sem("gu_copied")
        gu_turned = sem("gu_turned")
        silu_ready = sem("silu_ready")
        hid_ready = sem("hid_ready")
        out_a, out_b = sem("out_a"), sem("out_b")
        diag_ready = sem("diag_ready")
        spread_done = sem("spread_done")
        wstep, whalf, wsel_ready = sem("wstep"), sem("whalf"), sem("wsel_ready")
        sc_done = sem("sc_done")
        sc_added = sem("sc_added")
        last_added = sem("last_added")
        gfin_loaded = sem("gfin_loaded")
        spread_copied = sem("spread_copied")
        small_done = sem("small_done")
        fin_ss = [sem(f"fin_ss{t}") for t in range(3)]
        fin_rstd = [sem(f"fin_rstd{t}") for t in range(3)]
        fin_ready = sem("fin_ready")

        HALF = s5_half_steps()
        LATE = [HALF[j + 3] if j + 3 < NJ else HALF[-1] + 2 * (j + 4 - NJ) for j in range(NJ)]
        bu_at = {h: [j for j in range(NJ) if HALF[j] == h] for h in range(2 * len(TILES))}
        y_at = {h: [j for j in range(NJ) if LATE[j] == h] for h in range(2 * len(TILES))}
        TB = ((2, 3, 5, 6), (4, 7, 4, 7))
        YB = (4, 7)
        XB = (2, 3, 5, 6)
        OB = ((0, 1, 4), (5, 6, 7))
        FB = (5, 7)
        TR = [128, 128, 64]
        BU = [(2, 3), (5, 6)]
        (LR, LI, LDT, DT, X, TH, N_, R_, T1, T2, CARG, MAG, SI, CO, ABR, ABI, DEN, RDEN, FR, FI) = range(20)

        def pr(i):
            return prm[:, i, :]

        def st_count(c):
            return 2 * min(c, NCP) + 2 * SPC * max(c - NCP, 0)

        def h_last(ap):
            return ap[:, :, NPRE - 1:T:DSEQ]

        block = ctx.enter_context(nc.Block())

        def chunk_view(ap):
            return ap.rearrange("p h i -> p (h i)")

        @block.sync
        def _(sp):
            w_in = A["w_in"][0].rearrange("(p k) n -> p k n", k=KT)
            w_glu = A["w_glu"][0].rearrange("(k p) n -> p k n", p=128)
            w_out = A["w_out"][0].rearrange("(k p) n -> p k n", p=128)
            xp, xs = A["x_prompt"][0], A["x_sample"].rearrange("b t d -> (b t) d")

            def load_chunk(n):
                kind, i = CHUNKS[n]
                if n >= 2:
                    k0, i0 = CHUNKS[n - 2]
                    if k0 == "out":
                        sp.wait_ge(wout_done, 3 * (i0 + 1))
                    else:
                        sp.wait_ge(proj_done, TIDX[(k0, 2 * i0 + 1)] + 1)
                if kind == "glu":
                    src, dst = w_glu[:, :, 256 * i:256 * i + 256], ring[n % 2][:, 0:2048]
                elif kind == "out":
                    src, dst = w_out[:, :, 256 * i:256 * i + 256], ring[n % 2]
                else:
                    c0 = COL0[kind] + 256 * i
                    src, dst = w_in[:, :, c0:c0 + 256], ring[n % 2]
                sp.dma_start(dst.rearrange("p (k n) -> p k n", n=256), src).then_inc(ring_loaded[n % 2], 16)

            for r_, name in enumerate(("lam_re", "lam_im")):
                sp.dma_start(lam_ld[:, r_, :], A[name][0].rearrange("(j g) p -> j (g p)", g=2)).then_inc(lam_loaded, 16)
            sp.dma_start(xr[0:N_META, 0, :], A["meta"]).then_inc(x_loaded[0], 16)
            sp.dma_start(xr[N_META:XT_ROWS, 0, :], xp[0:96, :]).then_inc(x_loaded[0], 16)
            sp.dma_start(xr[:, 1, :], xp[96:208, :]).then_inc(x_loaded[1], 16)
            sp.dma_start(xr[0:48, 2, :], xp[208:256, :]).then_inc(x_loaded[2], 16)
            sp.dma_start(xr[48:112, 2, :], xs).then_inc(x_loaded[2], 16)
            load_chunk(0)
            for r_, name in enumerate(("state_s5_re", "state_s5_im")):
                src = A[name][0].rearrange("b (j g) p -> (b j) (g p)", g=2)
                for m in range(2):
                    sp.dma_start(st_ld[:, 2 * r_ + m, :], src[128 * m:128 * m + 128, :]).then_inc(s5_loaded, 16)
            for r_, name in enumerate(("s5_b_re", "s5_b_im")):
                src = A[name][0].rearrange("(j g) p c -> (g p) j c", g=2)
                sp.dma_start(b_ld[:, r_, :].rearrange("p (j c) -> p j c", c=GC), src).then_inc(s5_loaded, 16)
            load_chunk(1)
            for r_, name in enumerate(("s5_c_re", "s5_c_im")):
                src = A[name][0].rearrange("(c g) x p -> (g x) c p", g=8)
                sp.dma_start(c_ld[:, r_], src).then_inc(c_loaded, 16)
            for n in range(2, CIDX[("out", 2)]):
                load_chunk(n)
                if n == CIDX[("r", 0)]:
                    sp.wait_ge(rotated, 2 * NJ)
                    for s_ in range(SPC):
                        sp.dma_start(sstate[0][:, s_], A["state_gla"][0, s_].rearrange("h k v -> k h v"))\
                          .then_inc(ss_loaded[0], 16)
                if n == CIDX[("glu", 2)]:
                    sp.wait_ge(proj_done, TIDX[("glu", 0)])
                    for s_ in range(SPC):
                        sp.dma_start(sstate[1][:, s_], A["state_gla"][0, SPC + s_].rearrange("h k v -> k h v"))\
                          .then_inc(ss_loaded[1], 16)

            def expert_weights(e, first, pieces):
                for j in pieces:
                    if j < 8:
                        name, q, kt, n = ("w_gate", "w_up")[j % 2], j // 2, KT, HID
                    else:
                        name, q, kt, n = "w_down", j - 8, HID // 128, D
                    per = 2048 // n
                    src = A[name][0].rearrange("e (p k) n -> e p (k n)", k=kt)
                    if first is not None:
                        sp.wait_ge(weights_used, 12 * first + j - 11)
                    sp.dma_start(wpiece[j], src[bass.ds(e, 1), :, per * q * n:per * (q + 1) * n]
                                 .rearrange("e p n -> (e p) n")).then_inc(piece_loaded[j], 16)

            sp.wait_ge(st_added, 2 * st_count(NCH))
            sp.dma_start(A["new_gla_prompt"][0, 0].rearrange("h k v -> k h v"), S).then_inc(s_stored, 16)
            for i in range(2):
                sp.dma_start(A["new_gla_sample"][0, SPC * i:SPC * i + SPC].rearrange("s h k v -> k s h v"), sstate[i])\
                    .then_inc(states_stored, 16)
            for i in range(2, 8):
                load_chunk(CIDX[("out", i)])
                if i == 2:
                    sp.wait_ge(mix_gla, 2 * (NCH - 1))
                    sp.wait_ge(states_stored, 32)
                if i < 5:
                    expert_weights(0, None, range(4 * i - 8, 4 * i - 4))
            with sp.Fori(1, NE) as e:
                expert_weights(e, e, range(12))
            sp.wait_ge(small_done, 1)
            n_over = sp.value_load(novf[0:1, 0:1], min_val=0, max_val=NOP)
            with sp.Fori(0, NOP) as o:
                with sp.If(n_over > o):
                    for half in range(2):
                        e = sp.value_load(ovexp[0:1, bass.ds(2 * o + half, 1)], min_val=0, max_val=NE - 1)
                        expert_weights(e, 2 * o + (NE + half), range(12))
                sp.nop()
            outs = [A["y_prompt"][0, 0:128, :], A["y_prompt"][0, 128:256, :], A["y_sample"].rearrange("b t d -> (b t) d")]
            for t in range(3):
                sp.wait_ge(fin_ready, t + 1)
                sp.dma_start(outs[t], hn[0:TR[t], t, :]).then_inc(y_stored, 16)
            sp.wait_ge(y_stored, 48)

        @block.gpsimd
        def _(pool):
            gp = nc.gpsimd
            st = Steps(pool, pool_steps)

            def keep(ap, pattern, base, mult, count=masks_made):
                st.sync()
                return gp.affine_select(out=ap, in_=ap, compare_op=ALU.is_ge, fill=0.0, base=base,
                                        pattern=pattern, channel_multiplier=mult)

            st(gp.memset(ident, 1.0))
            st(keep(ident, [[-1, 128]], 0, 1))
            st.sync()
            keep(ident, [[1, 128]], 0, -1).then_inc(ident_made, 1)
            with nc.allow_non_contiguous_dma(reason="short per-channel vectors"):
                vecs = [
                    (ggla, A["g_gla"][0].rearrange("h (m p) -> p (h m)", p=128)),
                    (dsk, A["d_skip"][0].rearrange("(c g) x -> (g x) c", g=8)),
                    (bgk, A["b_gk"][0].rearrange("(h p) -> p h", p=128)),
                    (bglu, A["b_glu"][0].rearrange("(c p) -> p c", p=128)),
                    (wgk, A["w_gk2"][0]),
                    (wa, A["w_in"][0].rearrange("(p k) n -> p k n", k=KT)[:, :, OFF_A:OFF_A + RANK]),
                ]
                ldt = A["log_dt"][0].rearrange("(j g) -> g j", g=2)
                for g2 in range(2):
                    pool.dma_start(prm[64 * g2:64 * g2 + 64, LDT, :], ldt[g2:g2 + 1, :].broadcast_to([64, NJ]))\
                        .then_inc(ldt_loaded, 16)
                for dst, src in vecs:
                    pool.dma_start(dst, src).then_inc(small_loaded, 16)
            for m, w in ((cmaskP, CL), (cmaskS, DSEQ)):
                st(gp.memset(m, 1.0))
                st(keep(m, [[1, 128]], 0, -1))
                st(keep(m, [[-w, 128 // w], [0, w]], 0, 1))
            for m, w in ((hmask, CL), (hsmask, DSEQ)):
                st(gp.memset(m, 1.0))
                st(keep(m, [[-w, 128 // w]], 0, 1))
                st(keep(m, [[w, 128 // w]], w - 1, -1))
            st(gp.memset(qmask, 1.0))
            st(keep(qmask, [[-DSEQ, SPC], [1, CL]], 0, 0))
            st(keep(qmask, [[DSEQ, SPC], [-1, CL]], DSEQ - 1, 0))
            st(gp.memset(s5mask, 1.0))
            st(gp.memset(gmask32, 1.0))
            st(gp.memset(gmask8, 1.0))
            st.sync()
            st(gp.memset(s5mask[:, 0:1], 0.0))
            st(gp.memset(s5mask[:, NPRE:T:DSEQ], 0.0))
            st(gp.memset(gmask32[:, 0:384:CL], 0.0))
            st(gp.memset(gmask8[:, 0:256:DSEQ], 0.0))
            m8 = prm[:, 20, 0:8]
            par = prm[:, 20, 8:10]
            st(gp.memset(m8, 1.0))
            st(keep(m8, [[-GC, 8]], 0, 1))
            st(keep(m8, [[GC, 8]], GC - 1, -1))
            st.sync()
            p4 = prm[:, 20, 10:14]
            m8v = m8.rearrange("p (a g) -> p a g", g=2)
            st(gp.tensor_tensor(p4.rearrange("p (a g) -> p a g", g=2), m8v[:, 0:2], m8v[:, 2:4], ALU.add))
            st.sync()
            st(gp.tensor_tensor(par, p4[:, 0:2], p4[:, 2:4], ALU.add))
            for m in (qT, kT):
                st(gp.memset(m[:, 0, :, 0:PADT], 0.0))
            st(gp.memset(pad, 0.0))
            st.sync()
            pool.sem_inc(masks_made, 1)

            def mul(o, a, b):
                st(gp.tensor_tensor(o, a, b, ALU.mult))

            def add(o, a, b):
                st(gp.tensor_tensor(o, a, b, ALU.add))

            def sub(o, a, b):
                st(gp.tensor_tensor(o, a, b, ALU.subtract))

            pool.wait_ge(prm_ready, 1)
            pool.wait_ge(dt_ready, 1)
            mul(pr(X), pr(LR), pr(DT))
            mul(pr(TH), pr(LI), pr(DT))
            mul(pr(T1), pr(LR), pr(LR))
            mul(pr(T2), pr(LI), pr(LI))
            st.sync()
            gp.tensor_tensor(pr(DEN), pr(T1), pr(T2), ALU.add).then_inc(arg_ready, 1)
            st(gp.tensor_scalar(pr(N_), pr(TH), 1.0 / (2 * math.pi), MAGIC, ALU.mult, ALU.add))
            st.sync()
            st(gp.tensor_scalar(pr(N_), pr(N_), -MAGIC, None, ALU.add))
            st.sync()
            st(gp.tensor_scalar(pr(T1), pr(N_), TWO_PI_1, None, ALU.mult))
            st(gp.tensor_scalar(pr(T2), pr(N_), TWO_PI_2, None, ALU.mult))
            st.sync()
            sub(pr(R_), pr(TH), pr(T1))
            st.sync()
            st(gp.tensor_scalar(pr(T1), pr(N_), TWO_PI_3, None, ALU.mult))
            sub(pr(R_), pr(R_), pr(T2))
            st.sync()
            sub(pr(R_), pr(R_), pr(T1))
            st.sync()
            st(gp.tensor_scalar(pr(R_), pr(R_), 3.1415925, -3.1415925, ALU.min, ALU.max))
            st.sync()
            st(gp.tensor_scalar(pr(T1), pr(R_), 0.0, None, ALU.min))
            st(gp.tensor_scalar(pr(T2), pr(R_), 0.0, None, ALU.max))
            st.sync()
            sub(pr(T2), pr(T2), pr(T1))
            st.sync()
            gp.tensor_scalar(pr(CARG), pr(T2), -1.0, math.pi / 2, ALU.mult, ALU.add).then_inc(arg_ready, 1)
            pool.wait_ge(trig_ready, 3)
            mul(pr(ABR), pr(MAG), pr(CO))
            mul(pr(ABI), pr(MAG), pr(SI))
            st.sync()
            st(gp.tensor_scalar(pr(N_), pr(ABR), -1.0, None, ALU.add))
            mul(pr(T2), pr(ABI), pr(LI))
            mul(pr(FI), pr(ABI), pr(LR))
            st.sync()
            mul(pr(T1), pr(N_), pr(LR))
            mul(pr(FR), pr(N_), pr(LI))
            st.sync()
            sub(pr(FI), pr(FI), pr(FR))
            add(pr(T1), pr(T1), pr(T2))
            st.sync()
            pool.wait_ge(dt_ready, 2)
            mul(pr(FI), pr(FI), pr(RDEN))
            mul(pr(FR), pr(T1), pr(RDEN))
            st.sync()
            pool.wait_ge(s5_loaded, 16 * 6)
            tb = Region(arena, at_d + 1344 + 16, 1456)
            ta, tc = tb.take(NJ, GC), tb.take(NJ, GC)
            bv = [b_ld[:, r_, :].rearrange("p (j c) -> p j c", c=GC) for r_ in range(2)]
            fr, fi = (bc(pr(x).unsqueeze(2), 2, GC) for x in (FR, FI))
            for r_ in range(2):
                st.sync()
                mul(ta, fr, bv[r_])
                mul(tc, fi, bv[1 - r_])
                st.sync()
                padv = pad[:, r_].rearrange("p c (q g x) -> p (c q) g x", q=4, g=2)
                for g2 in range(2):
                    rows = slice(64 * g2, 64 * g2 + 64)
                    st(gp.tensor_tensor(padv[rows, :, g2, :], ta[rows], tc[rows], ALU.subtract if r_ == 0 else ALU.add))
            st.sync()
            pool.sem_inc(pad_ready, 1)
            pool.wait_ge(h0_ready, 1)
            tA, tB = (x.rearrange("p j c -> p (j c)")[:, 0:NSEQ * NJ].rearrange("p (b j) -> p b j", b=NSEQ) for x in (ta, tc))
            ar, ai = (bc(pr(x).unsqueeze(1), 1, NSEQ) for x in (ABR, ABI))
            for r_ in range(2):
                st.sync()
                mul(tA, ar, h0[:, r_])
                mul(tB, ai, h0[:, 1 - r_])
                st.sync()
                st(gp.tensor_tensor(ah0[:, r_].rearrange("p j b -> p b j"), tA, tB, ALU.subtract if r_ == 0 else ALU.add))
            tw = [x.rearrange("p j c -> p (j c)")[:, 256 * i:256 * i + 256] for x in (ta, tc) for i in range(2)]

            def cmul(o, a, e, w):
                t = [x[:, 0:NJ * w].rearrange("p (j w) -> p j w", w=w) for x in tw]
                er, ei = (bc(x.unsqueeze(2), 2, w) for x in e)
                st.sync()
                mul(t[0], a[0], er)
                mul(t[1], a[1], ei)
                mul(t[2], a[0], ei)
                mul(t[3], a[1], er)
                st.sync()
                sub(o[0], t[0], t[1])
                add(o[1], t[2], t[3])

            def cols(tab, a, b):
                return tab[:, 0, :, a:b], tab[:, 1, :, a:b]

            for tab in (Bt, At):
                st(gp.memset(tab[:, 0, :, 0:1], 1.0))
                st(gp.memset(tab[:, 1, :, 0:1], 0.0))
            e = (pr(CO), pr(SI))
            e2 = [(pr(T1), pr(T2)), (pr(X), pr(TH))]
            st.sync()
            st(gp.tensor_copy(Bt[:, 0, :, 1:2], e[0].unsqueeze(2)))
            st(gp.tensor_copy(Bt[:, 1, :, 1:2], e[1].unsqueeze(2)))
            for lvl, (tab, w) in enumerate([(Bt, 2), (Bt, 4), (Bt, 8), (At, 1), (At, 2), (At, 4), (At, 8), (At, 16)]):
                n = e2[lvl % 2]
                cmul(tuple(x.unsqueeze(2) for x in n), tuple(x.unsqueeze(2) for x in e), e, 1)
                e = n
                hi = min(2 * w, tab.shape[3])
                cmul(cols(tab, w, hi), cols(tab, 0, hi - w), e, hi - w)
            st.sync()
            pool.sem_inc(tables_ready, 1)
            pool.wait_ge(c_loaded, 32)
            pool.wait_ge(pad_turned, 4)
            for r_ in range(2):
                pv = pad[:, r_].rearrange("p c (g x) -> p c g x", g=2)
                for g2 in range(2):
                    st(gp.tensor_scalar(pv[:, :, g2, :], c_ld[:, r_], par[:, g2:g2 + 1], 1.0 if r_ == 0 else -1.0,
                                        ALU.mult, ALU.mult))
            st.sync()
            pool.sem_inc(pad_ready, 1)

            pool.wait_ge(xn_turned, 12)
            for hf in range(2):
                st(gp.memset(vT[:, hf, 0, :].rearrange("p (h i) -> p h i", i=CL)[:, :, 0:PADT], 0.0))
            st.sync()
            pool.sem_inc(masks_made, 1)

            for j in range(NJ):
                c, q = j // 4, j % 4
                cs, sn = (bc(E[c % 2][:, r_:r_ + 1, q, :], 1, 2) for r_ in range(2))
                g_, q1 = Gs[j % 2], Q1[j % 2]
                pool.wait_ge(scanned, 2 * (j + 1))
                if j >= 2:
                    pool.wait_ge(h_used, j - 1)
                    pool.wait_ge(hl_saved, j - 1)
                if j:
                    pool.wait_ge(rotated, 2 * j)
                st.sync()
                mul(q1, cs, g_)
                mul(Q2, sn, g_)
                st.sync()
                gp.tensor_tensor(q1[:, 0], q1[:, 0], Q2[:, 1], ALU.subtract).then_inc(rotated, 1)
                gp.tensor_tensor(q1[:, 1], q1[:, 1], Q2[:, 0], ALU.add).then_inc(rotated, 1)
            pool.wait_ge(pad_turned, 8)
            gp.memset(S, 0.0).then_inc(masks_made, 1)
            pool.wait_ge(hl_copied, 2)
            for r_, name in enumerate(("re", "im")):
                pool.dma_start(A[f"new_s5_{name}_prompt"].rearrange("l b (j g) p -> (l b j) (g p)", g=2),
                               hlT[0:NJ, 3 * r_, :]).then_inc(stores, 16)
                dst = A[f"new_s5_{name}_sample"].rearrange("l b (j g) p -> (l b j) (g p)", g=2)
                for m in range(2):
                    pool.dma_start(dst[128 * m:128 * m + 128, :], hlT[:, 3 * r_ + 1 + m, :]).then_inc(stores, 16)
            pool.wait_ge(st_added, 2 * st_count(NCH))
            pool.wait_ge(mix_s5, 8)
            pool.wait_ge(s_stored, 16)
            pool.dma_start(hrow[:, 0, :], A["x_prompt"][0, 0:128, :]).then_inc(res_loaded, 16)
            pool.dma_start(hrow[:, 1, :], A["x_prompt"][0, 128:256, :]).then_inc(res_loaded, 16)
            pool.dma_start(hrow[0:NS, 2, :], A["x_sample"].rearrange("b t d -> (b t) d")).then_inc(res_loaded, 16)
            pool.wait_ge(stores, 6 * 16)
            pool.dma_start(gffn, A["g_ffn"].broadcast_to([128, D])).then_inc(ffn_loaded, 16)
            pool.dma_start(wrg_ld, A["w_rg"][0].rearrange("(p k) g -> p k g", k=KT)).then_inc(ffn_loaded, 16)
            pool.dma_start(wre_ld, A["w_re"][0].rearrange("g (p k) e -> p g k e", k=KT)).then_inc(ffn_loaded, 16)
            pool.dma_start(br[:, 0:NG], A["b_rg"].broadcast_to([128, NG])).then_inc(ffn_loaded, 16)
            pool.dma_start(br[:, NG:], A["b_re"].rearrange("l g e -> l (g e)").broadcast_to([128, NE])).then_inc(ffn_loaded, 16)
            pool.wait_ge(ffn_loaded, 80)
            gp.tensor_copy(Wr[:, :, 0:NG], wrg_ld).then_inc(wr_ready, 1)
            for g_ in range(NG):
                gp.tensor_copy(Wr[:, :, NG + EPG * g_:NG + EPG * g_ + EPG], wre_ld[:, g_]).then_inc(wr_ready, 1)
            pool.wait_ge(wr_ready, 5)
            st(gp.memset(hn[NS:, 2, :], 0.0))
            st.sync()
            pool.wait_ge(wout_done, 24)
            st(gp.memset(ones, 1.0))
            st(gp.memset(tri, 1.0))
            st(gp.memset(Lg, 0.0))
            st(gp.memset(lg8, -BIG))
            st(gp.memset(ssum, 1.0))
            st(gp.iota(sloti, pattern=[[1, 2 * CAP]], base=0, channel_multiplier=0))
            st(gp.iota(slotpi, pattern=[[0, 1]], base=0, channel_multiplier=1))
            st.sync()
            st(gp.affine_select(out=tri, in_=tri, compare_op=ALU.is_ge, fill=0.0, base=-1, pattern=[[1, 128]],
                                channel_multiplier=-1))
            st(gp.iota(iota32i, pattern=[[1, NE]], base=0, channel_multiplier=0))
            st.sync()
            st(gp.tensor_copy(iota32, iota32i))
            st(gp.tensor_copy(slot, sloti))
            st(gp.tensor_copy(slotp, slotpi))
            st.sync()
            pool.sem_inc(rconst, 1)
            pool.wait_ge(hn_ready, 3)
            pool.dma_start(gfin, A["g_final"].rearrange("(a d) -> a d", a=1).broadcast_to([128, D])).then_inc(gfin_loaded, 16)

        @block.scalar
        def _(act):
            sc = nc.scalar
            st = Steps(act, act_steps)
            act.dma_start(gmix, A["g_mix"][0].rearrange("(p k) -> p k", k=KT)).then_inc(gmix_loaded, 16)

            act.wait_ge(ident_made, 1)

            def load_table(func):
                st.sync()
                st(sc.activation(warm, ident[0:1, 0:1], func))

            load_table(ACT.Sqrt)

            def square(t):
                act.wait_ge(x_loaded[t], (32, 16, 32)[t])
                ejunk = arena[0:XT_ROWS, D * t:D * t + D]
                sc.activation(ejunk, xr[:, t, :], ACT.Square, accum_out=xss[0:XT_ROWS, 0, t:t + 1]).then_inc(xn_sq, 1)

            def root(t):
                act.wait_ge(xn_mean, t + 1)
                sc.activation(xss[0:XT_ROWS, 0, t:t + 1], xss[0:XT_ROWS, 0, t:t + 1], ACT.Sqrt).then_inc(xn_sqrt, 1)

            square(0)
            root(0)
            square(1)
            root(1)
            square(2)
            root(2)
            act.wait_ge(xn_rstd, 2)
            sc.activation(xr[:, 1, :], xr[:, 1, :], ACT.Copy, scale=xss[0:XT_ROWS, 1, 1:2]).then_inc(xn_scaled[1], 1)
            act.wait_ge(prm_turned, 1)
            sc.activation(prm[:, LR:LI + 1, :], ps[:, 4, 0:2 * NJ].rearrange("p (a j) -> p a j", a=2), ACT.Copy)\
              .then_inc(prm_ready, 1)
            act.wait_ge(ldt_loaded, 32)
            sc.activation(pr(DT), pr(LDT), ACT.Exp).then_inc(dt_ready, 1)
            act.wait_ge(prm_turned, 2)
            act.wait_ge(xn_turned, 12)
            sc.activation(h0.rearrange("p r b j -> p (r b j)"), ps[:, 7, :], ACT.Copy).then_inc(h0_ready, 1)
            act.wait_ge(arg_ready, 2)
            sc.activation(pr(MAG), pr(X), ACT.Exp).then_inc(trig_ready, 1)
            sc.activation(pr(SI), pr(R_), ACT.Sin).then_inc(trig_ready, 1)
            sc.activation(pr(CO), pr(CARG), ACT.Sin).then_inc(trig_ready, 1)

            def turn_copies(k):
                dst = (BT, CT)[k]
                for i in range(4):
                    act.wait_ge(pad_turned, 4 * k + i + 1)
                    out = dst[:, i // 2, 4 * (i % 2):4 * (i % 2) + 4, :].rearrange("p c x -> p (c x)")
                    sc.activation(out, ps[:, TB[k][i], :], ACT.Copy).then_inc((bt_ready, ct_ready)[k], 1)

            def decay(j):
                if j == 0:
                    act.wait_ge(trig_ready, 3)
                    act.wait_ge(masks_made, 1)
                if j >= 2:
                    act.wait_ge(scanned, 2 * (j - 1))
                sc.activation(dec[j % 2], s5mask, ACT.Copy, scale=prm[:, MAG, j:j + 1]).then_inc(dec_ready, 1)

            def keep_last(j):
                act.wait_ge(rotated, 2 * (j + 1))
                sc.activation(hl[:, :, :, j], h_last(Q1[j % 2]), ACT.Copy).then_inc(hl_saved, 1)

            def evacuate(p):
                kind, i = TILES[p]
                act.wait_ge(proj_done, p + 1)
                src = ps[:, p % 2, 0:T]
                if kind == "u":
                    sc.activation(uT[:, i, :], src, ACT.Copy).then_inc(proj_read, 1)
                elif kind == "a":
                    act.wait_ge(xn_turned, 12)
                    sc.activation(aT, ps[0:RANK, p % 2, 0:T], ACT.Copy).then_inc(proj_read, 1)
                elif kind in "qkv":
                    if kind == "v" and i == 0:
                        act.wait_ge(xn_turned, 12)
                    if kind == "v":
                        h_, dst = i // 2, vT[:, i % 2].rearrange("p c (h i) -> p c h i", i=CL)
                    else:
                        h_, dst = i, qT if kind == "q" else kT
                    scale = DK ** -0.5 if kind == "q" else 1.0
                    st(sc.activation(dst[:, 0, h_, PADT:CL], src[:, 0:N_META], ACT.Copy, scale=scale))
                    sc.activation(dst[:, 1:, h_, :], src[:, N_META:].rearrange("p (c i) -> p c i", i=CL), ACT.Copy,
                                  scale=scale).then_inc(proj_read, 1)
                elif kind == "gk":
                    act.wait_ge(scanned, 2 * NJ)
                    st(sc.activation(bG[:, 0, i, PADT:CL], src[:, 0:N_META], ACT.Identity, bias=bgk[:, i:i + 1]))
                    sc.activation(bG[:, 1:, i, :], src[:, N_META:].rearrange("p (c i) -> p c i", i=CL), ACT.Identity,
                                  bias=bgk[:, i:i + 1]).then_inc(proj_read, 1)
                elif kind == "r":
                    sc.activation(rT[:, i, :], src[:, 0:TO], ACT.Silu).then_inc(proj_read, 1)
                else:
                    if i >= 2:
                        act.wait_ge(mix_s5, i - 1)
                    sc.activation(glu_t[i % 2], src[:, 0:TO], ACT.Sigmoid, bias=bglu[:, i:i + 1]).then_inc(proj_read, 1)

            def gates():
                act.wait_ge(rotated, 2 * NJ)
                act.wait_ge(proj_read, TIDX[("gk", 3)] + 1)
                act.wait_ge(gate_b, 1)
                flat = [x.rearrange("p c h i -> p (c h i)") for x in (bG, eb, en)]
                sc.activation(flat[2], flat[0], ACT.Abs).then_inc(gate_abs, 1)
                act.wait_ge(gate_abs, 1)
                sc.activation(flat[2], flat[2], ACT.Exp, scale=-1.0).then_inc(gate_abs, 1)
                act.wait_ge(gate_abs, 2)
                sc.activation(flat[2], flat[2], ACT.Ln, bias=1.0).then_inc(gate_abs, 1)
                act.wait_ge(gate_b, 3)
                sc.activation(flat[1], flat[0], ACT.Exp, scale=1.0 / 16).then_inc(gate_exp, 1)
                sc.activation(flat[2], flat[2], ACT.Exp, scale=-1.0 / 16).then_inc(gate_exp, 1)
                act.wait_ge(gate_b, 5)
                sc.activation(flat[0], flat[0], ACT.Exp, scale=1.0 / 16).then_inc(gate_exp, 1)

            def copy_v(c):
                act.wait_ge(front_done, c + 1)
                if c >= 2:
                    act.wait_ge(st_done, st_count(c - 1))
                sc.activation(Vn[c % 2], ps[:, 4, 0:DV], ACT.Copy).then_inc(v_copied, 1)

            def read_o(c):
                if c >= 1:
                    act.wait_ge(o_done, c)
                    st(sc.activation(junk, ps[:, 6, 0:DV], ACT.Square, accum_out=gss[:, c - 1:c]))
                    sc.activation(o_all[:, c - 1, :], ps[:, 6, 0:DV], ACT.Copy).then_inc(o_read, 1)

            def scale_o(chunks):
                for c in chunks:
                    sc.activation(o_all[:, c, :], o_all[:, c, :], ACT.Copy, scale=gss[:, 16 + c:17 + c]).then_inc(o_scaled, 1)

            assert GLA_TILE0 + NCH - 1 == TIDX[("glu", 4)]
            for p in range(len(TILES)):
                if p == PAD_B_TILE:
                    turn_copies(0)
                if p == PAD_C_TILE:
                    turn_copies(1)
                for h_ in (2 * p, 2 * p + 1):
                    for j in bu_at[h_]:
                        decay(j)
                    for j in y_at[h_]:
                        keep_last(j)
                if p == TIDX[("r", 6)]:
                    act.wait_ge(y_read, 8)
                    sc.activation(zT.rearrange("p c t -> p (c t)"), zT.rearrange("p c t -> p (c t)"),
                                  ACT.Gelu_apprx_tanh).then_inc(z_ready, 1)
                c = p - GLA_TILE0
                if 0 <= c < NCH:
                    copy_v(c)
                if TILES[p] == ("glu", 5):
                    act.wait_ge(o_sqrt, 1)
                    sc.activation(gss[:, 0:NCH - 1], gss[:, 0:NCH - 1], ACT.Sqrt).then_inc(o_sqrt, 1)
                evacuate(p)
                if TILES[p] == ("glu", 6):
                    act.wait_ge(o_rstd, 1)
                    scale_o(range(5))
                if TILES[p] == ("glu", 7):
                    scale_o(range(5, NCH - 1))
                if TILES[p] == ("gk", 3):
                    gates()
                if 0 <= c < NCH:
                    read_o(c)
            for i in range(2):
                act.wait_ge(hl_turned, i + 1)
                sc.activation(hlT[:, 3 * i:3 * i + 3, :], ps[:, 2 + i, 0:384].rearrange("p (a b) -> p a b", b=128),
                              ACT.Copy).then_inc(hl_copied, 1)
            load_table(ACT.Sqrt)
            for i in range(8):
                for t in range(3):
                    act.wait_ge(h_added, 3 * i + t + 1)
                    if 3 * i + t:
                        act.wait_ge(h_ss, 3 * i + t)
                    sc.activation(hjunk[0:TR[t]], hrow[0:TR[t], t, 256 * i:256 * i + 256], ACT.Square,
                                  accum_out=ssp[0:TR[t], t, i:i + 1]).then_inc(h_ss, 1)
            act.wait_ge(h_rstd, 1)
            sc.activation(ssum[:, 0:3], ssum[:, 0:3], ACT.Sqrt).then_inc(h_rstd, 1)
            for n in range(12):
                t, g_ = n // 4, n % 4
                act.wait_ge(hn_turned, n + 1)
                sc.activation(hnT[:, 4 * g_:4 * g_ + 4, 128 * t:128 * t + TR[t]],
                              ps[:, XB[n % 4], 0:4 * TR[t]].rearrange("p (k t) -> p k t", k=4), ACT.Copy).then_inc(hnT_ready, 1)
            load_table(ACT.Exp)
            act.wait_ge(logits_done, 1)
            sc.activation(logT[:, 1], ps[64:64 + NL, 7, 0:TO], ACT.Copy).then_inc(logitsT_ready, 1)
            for i in range(2):
                act.wait_ge(ex_in, i + 1)
                x_ = (x4.rearrange("p t g -> p (t g)"), x1.rearrange("p t g -> p (t g)"))[i]
                sc.activation(x_, x_, ACT.Exp).then_inc(ex_out, 1)

            def expert(m, half, inputs):
                n = 2 * m + half
                if inputs is not None:
                    x_parts(inputs)
                if isinstance(n, int) and n == 0:
                    act.wait_ge(small_done, 1)
                act.wait_ge(gu_turned, n + 1)
                gt = ps[:, 1, :].rearrange("p (k x t) -> p k x t", k=4, x=2)
                sc.activation(Hs, gt[:, :, 0, :], ACT.Silu).then_inc(silu_ready, 1)
                act.wait_ge(weights_used, 12 * (n + 1))
                if not (isinstance(m, int) and m == 0):
                    act.wait_ge(sc_done, 6 * m)
                for x in range(2):
                    sc.activation(Os[CAP * half:CAP * half + CAP, 512 * x:512 * x + 512],
                                  ps[CAP * x:CAP * x + CAP, 6, :], ACT.Copy).then_inc(out_a, 1)

            def x_parts(m):
                for i in (0, 2):
                    act.wait_ge(x_turned, 4 * m + i + 1)
                    sc.activation(xT[:, 4 * i:4 * i + 4].rearrange("p k t -> p (k t)"), ps[:, 2, :], ACT.Copy)\
                        .then_inc(xT_a, 1)

            load_table(ACT.Silu)
            expert(0, 0, 0)
            expert(0, 1, 1)
            with act.Fori(1, NPAIR - 1) as m:
                expert(m, 0, None)
                expert(m, 1, m + 1)
            expert(NPAIR - 1, 0, None)
            expert(NPAIR - 1, 1, None)
            n_over = act.value_load(novf[0:1, 0:1], min_val=0, max_val=NOP)
            with act.Fori(0, NOP) as o:
                with act.If(n_over > o):
                    expert(o + NPAIR, 0, o + NPAIR)
                    expert(o + NPAIR, 1, None)
                act.nop()
            load_table(ACT.Sqrt)
            for t in range(3):
                act.wait_ge(last_added, 2 * (t + 1))
                sc.activation(hn[0:TR[t], t, :], hrow[0:TR[t], t, :], ACT.Square, accum_out=ssum[0:TR[t], 8 + t:9 + t])\
                  .then_inc(fin_rstd[t], 1)
                act.wait_ge(fin_ss[t], 1)
                sc.activation(ssum[0:TR[t], 8 + t:9 + t], ssum[0:TR[t], 8 + t:9 + t], ACT.Sqrt).then_inc(fin_rstd[t], 1)

        @block.vector
        def _(dve):
            ve = nc.vector
            st = Steps(dve, dve_steps)
            def root_inverse(t):
                v = xss[0:XT_ROWS, 0, t:t + 1]
                dve.wait_ge(xn_sq, t + 1)
                ve.tensor_scalar(v, v, 1.0 / D, EPS, ALU.mult, ALU.add).then_inc(xn_mean, 1)
                dve.wait_ge(xn_sqrt, t + 1)
                ve.reciprocal(xss[0:XT_ROWS, 1, t:t + 1], v).then_inc(xn_rstd, 1)

            def scale(t):
                dve.wait_ge(xn_rstd, t + 1)
                ve.tensor_scalar(xr[:, t, :], xr[:, t, :], xss[0:XT_ROWS, 1, t:t + 1], None, ALU.mult).then_inc(xn_scaled[t], 1)

            root_inverse(0)
            scale(0)
            root_inverse(1)
            root_inverse(2)
            scale(2)
            dve.wait_ge(gmix_loaded, 16)
            for n in range(12):
                t, g = n // 4, n % 4
                dve.wait_ge(xn_turned, n + 1)
                ve.tensor_tensor(xnT[:, 4 * g:4 * g + 4, XT_ROWS * t:XT_ROWS * t + XT_ROWS],
                                 ps[:, XB[n % 4], 0:4 * XT_ROWS].rearrange("p (k t) -> p k t", k=4),
                                 bc(gmix[:, 4 * g:4 * g + 4].unsqueeze(2), 2, XT_ROWS), ALU.mult).then_inc(xn_ready, 1)
            dve.wait_ge(arg_ready, 1)
            ve.reciprocal(pr(RDEN), pr(DEN)).then_inc(dt_ready, 1)

            def tables(c):
                e = E[c % 2]
                if c >= 2:
                    dve.wait_ge(rotated, 8 * (c - 1))
                a = [bc(At[:, r_, 4 * c:4 * c + 4, :].unsqueeze(3), 3, 16) for r_ in range(2)]
                b = [bc(Bt[:, r_, 4 * c:4 * c + 4, :].unsqueeze(2), 2, 17) for r_ in range(2)]
                if c:
                    dve.wait_ge(scanned, 8 * c - 4)
                    st.sync()
                ev = [e[:, r_, :, 0:NPRE].rearrange("p j (a b) -> p j a b", b=16) for r_ in range(2)]
                for r_, (x, y, op) in enumerate(((1, 1, ALU.subtract), (1, 0, ALU.add))):
                    st(ve.tensor_tensor(ev[r_], a[0], b[0 if r_ == 0 else 1], ALU.mult))
                    st(ve.tensor_tensor(ets, a[x], b[y], ALU.mult))
                    st.sync()
                    st(ve.tensor_tensor(ev[r_], ev[r_], ets, op))
                    st.sync()
                for r_ in range(2):
                    st(ve.tensor_copy(e[:, r_, :, NPRE:T].rearrange("p j (s t) -> p j s t", t=DSEQ),
                                      bc(e[:, r_, :, 0:DSEQ].unsqueeze(2), 2, NSEQ)))
                st.sync()

            def forward(j):
                c, q = j // 4, j % 4
                cs, sn = (bc(E[c % 2][:, r_:r_ + 1, q, :], 1, 2) for r_ in range(2))
                bu = ps[:, BU[j % 2][0]:BU[j % 2][1] + 1, 0:T]
                if j:
                    dve.wait_ge(scanned, 2 * j)
                st.sync()
                dve.wait_ge(bu_done, 2 * (j + 1))
                st(ve.tensor_tensor(P1, cs, bu, ALU.mult))
                ve.tensor_tensor(P2, sn, bu, ALU.mult).then_inc(bu_read, 1)
                st.sync()
                dve.wait_ge(bu_read, j + 1)
                st(ve.tensor_tensor(P1[:, 0], P1[:, 0], P2[:, 1], ALU.add))
                st(ve.tensor_tensor(P1[:, 1], P1[:, 1], P2[:, 0], ALU.subtract))
                st.sync()
                first = P1[:, :, NPRE:T:DSEQ]
                st(ve.tensor_tensor(first, first, ah0[:, :, j, :], ALU.add))
                dve.wait_ge(dec_ready, j + 1)
                if j >= 2:
                    dve.wait_ge(rotated, 2 * (j - 1))
                st.sync()
                for r_ in range(2):
                    ve.tensor_tensor_scan(Gs[j % 2][:, r_], dec[j % 2], P1[:, r_], 0.0, ALU.mult, ALU.add)\
                      .then_inc(scanned, 1)

            def read_y(c):
                dve.wait_ge(h_used, 4 * (c + 1))
                ve.scalar_tensor_tensor(out=zT[:, c, :], in0=uT[:, c, N_META:T], scalar=dsk[:, c:c + 1],
                                        in1=ps[:, YB[c % 2], 0:TO], op0=ALU.mult, op1=ALU.add).then_inc(y_read, 1)

            dve.wait_ge(tables_ready, 1)
            tables(0)
            for j in range(NJ):
                if j % 4 == 2 and j < NJ - 4:
                    tables(j // 4 + 1)
                forward(j)
                if j % 4 == 2 and j >= 6:
                    read_y(j // 4 - 1)
            read_y(7)

            def flat(x):
                return x.rearrange("p c h i -> p (c h i)")
            dve.wait_ge(proj_read, TIDX[("gk", 3)] + 1)
            ve.memset(bG[:, 0, :, 0:PADT], 0.0).then_inc(gate_b, 1)
            dve.wait_ge(gate_abs, 3)
            dve.wait_ge(gate_b, 1)
            st(ve.scalar_tensor_tensor(out=flat(bG), in0=flat(bG), scalar=0.0, in1=flat(en), op0=ALU.min, op1=ALU.subtract))
            st.sync()
            st(ve.memset(bG[:, 0, :, 0:PADT], 0.0))
            st.sync()
            bf = flat(bG)
            npf = NCP * H * CL
            for i in range(3):
                st(ve.tensor_tensor_scan(bf[:, 384 * i:384 * i + 384], gmask32, bf[:, 384 * i:384 * i + 384], 0.0,
                                         ALU.mult, ALU.add))
            st(ve.tensor_tensor_scan(bf[:, npf:], gmask8, bf[:, npf:], 0.0, ALU.mult, ALU.add))
            st.sync()
            st(ve.tensor_scalar(flat(en), bf, -80.0 * 16, None, ALU.max))
            st.sync()
            dve.sem_inc(gate_b, 1)
            dve.sem_inc(gate_b, 1)
            dve.wait_ge(gate_exp, 1)
            dve.wait_ge(rotated, 2 * NJ)
            bp = bG[:, 0:NCP].rearrange("p c h i -> p (c h) i")
            bs = bG[:, NCP:].rearrange("p c h (s t) -> p (c h s) t", t=DSEQ)
            lastp, lasts = (glast[:, 0:36].unsqueeze(2), glast[:, 36:68].unsqueeze(2))
            st(ve.tensor_copy(lastp, bp[:, :, CL - 1:CL]))
            st(ve.tensor_copy(lasts, bs[:, :, DSEQ - 1:DSEQ]))
            st.sync()
            ve.tensor_tensor(bp, bc(lastp, 2, CL), bp, ALU.subtract).then_inc(gate_b, 1)
            ve.tensor_tensor(bs, bc(lasts, 2, DSEQ), bs, ALU.subtract).then_inc(gate_b, 1)
            ve.tensor_tensor(flat(qT), flat(qT), flat(eb), ALU.mult).then_inc(gates_ready, 1)
            dve.wait_ge(gate_exp, 3)
            ve.tensor_tensor(flat(en), flat(en), flat(kT), ALU.mult).then_inc(gates_ready, 1)
            dve.wait_ge(gates_ready, 2)
            ve.tensor_tensor(flat(kT), flat(kT), flat(bG), ALU.mult).then_inc(gates_ready, 1)

            def front(c):
                f = FB[c % 2]
                sample = c >= NCP
                n = H * SPC if sample else H
                dve.wait_ge(front_done, c + 1)
                if c == 0:
                    dve.wait_ge(hl_saved, NJ)
                if c >= 1:
                    dve.wait_ge(st_done, st_count(c))
                ve.tensor_tensor(PTm[c % 2], ps[:, f, 384:512], cmaskS if sample else cmaskP, ALU.mult)\
                  .then_inc(front_ready, 1)
                if sample:
                    qv = qT[:, c].unsqueeze(2)
                    for h_ in range(H):
                        st(ve.tensor_tensor(qexp[:, h_], bc(qT[:, c, h_:h_ + 1, :], 1, SPC), qmask, ALU.mult))
                    st.sync()
                ve.tensor_tensor(Kexp[:, 0:n], bc(ps[:, f, 256:384].unsqueeze(1), 1, n),
                                 bc((hsmask if sample else hmask).unsqueeze(2), 2, 128), ALU.mult)\
                  .then_inc(front_ready, 1)

            def add_states(c):
                n = 2 * SPC if c >= NCP else 2
                for i in range(n):
                    dve.wait_ge(st_done, st_count(c) + i + 1)
                    for x in range(2):
                        src = ps[:, 2 + i % 2, 256 * x:256 * x + 256]
                        if c < NCP:
                            h_ = 2 * i + x
                            dst, dcol = S[:, h_], eb[:, c, h_, CL - 1:CL]
                        else:
                            s_, h_ = i // 2, 2 * (i % 2) + x
                            dst = sstate[c - NCP][:, s_, h_]
                            dcol = eb[:, c, h_, DSEQ * s_ + DSEQ - 1:DSEQ * s_ + DSEQ]
                        if c == 0 and i == 0 and x == 0:
                            dve.wait_ge(masks_made, 3)
                        if x == 0 and c >= 1:
                            dve.wait_ge(st_added, 2 * st_count(c))
                        ve.scalar_tensor_tensor(out=dst, in0=dst, scalar=dcol, in1=src, op0=ALU.mult, op1=ALU.add)\
                          .then_inc(st_added, 1)

            def gate_s5(c):
                dve.wait_ge(proj_read, TIDX[("glu", c)] + 1)
                dve.wait_ge(z_ready, 1)
                ve.tensor_tensor(mixT[:, 8 + c, :], glu_t[c % 2], zT[:, c, :], ALU.mult).then_inc(mix_s5, 1)

            for c in range(NCH):
                front(c)
                add_states(c)
                p = GLA_TILE0 + c
                if p < len(TILES) and TILES[p][0] == "glu":
                    gate_s5(TILES[p][1])
            dve.wait_ge(o_read, NCH - 1)
            g10 = gss[:, 0:NCH - 1]
            ve.tensor_scalar(g10, g10, 1.0 / DV, EPS, ALU.mult, ALU.add).then_inc(o_sqrt, 1)
            gate_s5(5)
            dve.wait_ge(o_sqrt, 2)
            ve.reciprocal(gss[:, 16:16 + NCH - 1], g10).then_inc(o_rstd, 1)
            dve.wait_ge(proj_read, TIDX[("r", 7)] + 1)
            st(ve.tensor_tensor(rT, rT, bc(ggla.unsqueeze(2), 2, TO), ALU.mult))
            gate_s5(6)
            gate_s5(7)
            st.sync()
            for c in range(NCH - 1):
                for hf in range(2):
                    n = 2 * c + hf
                    dve.wait_ge(o_turned, n + 1)
                    dst = mixT[:, hf:8:2, CL * c:CL * c + CL]
                    ve.tensor_tensor(dst, ps[:, XB[n % 4], 0:128].rearrange("p (h i) -> p h i", i=CL),
                                     rT[:, hf:8:2, CL * c:CL * c + CL], ALU.mult).then_inc(mix_gla, 1)
            dve.wait_ge(res_loaded, 48)
            for i in range(8):
                for t in range(3):
                    dve.wait_ge(wout_done, 3 * i + t + 1)
                    if t < 2:
                        d_ = hrow[:, t, 256 * i:256 * i + 256]
                        ve.tensor_tensor(d_, d_, ps[:, OB[i % 2][t], 0:256], ALU.add).then_inc(h_added, 1)
                    else:
                        d_ = hrow[0:NS, t, 256 * i:256 * i + 128]
                        st(ve.tensor_tensor(d_, d_, ps[0:NS, OB[i % 2][t], 0:128], ALU.add))
                        d_ = hrow[0:NS, t, 256 * i + 128:256 * i + 256]
                        ve.tensor_tensor(d_, d_, ps[NS:2 * NS, OB[i % 2][t], 0:128], ALU.add).then_inc(h_added, 1)
            dve.wait_ge(rconst, 1)
            st(ve.tensor_copy(tri16, tri))
            st(ve.tensor_copy(ones16, ones))
            dve.wait_ge(h_ss, 24)
            for t in range(3):
                st(ve.tensor_reduce(ssum[0:TR[t], t:t + 1], ssp[0:TR[t], t, :], AX.X, ALU.add))
            st.sync()
            ve.tensor_scalar(ssum[:, 0:3], ssum[:, 0:3], 1.0 / D, EPS, ALU.mult, ALU.add).then_inc(h_rstd, 1)
            dve.wait_ge(h_rstd, 2)
            st(ve.reciprocal(ssum[:, 4:7], ssum[:, 0:3]))
            st.sync()
            dve.wait_ge(ffn_loaded, 80)
            dve.wait_ge(wr_ready, 5)
            for t in range(3):
                rr = slice(0, TR[t])
                ve.scalar_tensor_tensor(out=hn[rr, t, :], in0=hrow[rr, t, :], scalar=ssum[rr, 4 + t:5 + t],
                                        in1=gffn[rr], op0=ALU.mult, op1=ALU.mult).then_inc(hn_ready, 1)
            dve.wait_ge(logitsT_ready, 1)
            ve.tensor_tensor(logT[:, 0], logT[:, 1], ps[0:NL, 7, 0:TO], ALU.add).then_inc(logitsT_ready, 1)
            dve.wait_ge(logits_turned, 1)
            for t in range(3):
                rr = slice(0, TR[t])
                st(ve.tensor_tensor(Lg[rr, t, :], ps[rr, 4, NL * t:NL * t + NL], br[rr], ALU.add))
            st.sync()
            st(ve.tensor_copy(lg8[:, :, 0:NG], Lg[:, :, 0:NG]))
            st.sync()
            for t in range(3):
                st(ve.max(gmx[:, t, :], lg8[:, t, :]))
            st.sync()
            for t in range(3):
                st(ve.max_index(gix[:, t, :], gmx[:, t, :], lg8[:, t, :]))
            ve.tensor_tensor(x4, Lg[:, :, 0:NG], bc(gmx[:, :, 0:1], 2, NG), ALU.subtract).then_inc(ex_in, 1)
            st.sync()
            st(ve.tensor_copy(gidx, gix[:, :, 0:1]))
            st.sync()
            st(ve.tensor_tensor(ohg, bc(iota32[:, 0:NG].unsqueeze(1), 1, 3), bc(gidx, 2, NG), ALU.is_equal))
            st.sync()
            for t in range(3):
                st(ve.tensor_tensor(lem[:, t], Lg[:, t, NG:].rearrange("p (g e) -> p g e", g=NG),
                                    bc(ohg[:, t, :].unsqueeze(2), 2, EPG), ALU.mult))
            st.sync()
            for t in range(3):
                st(ve.tensor_reduce(lsel[:, t, :], lem[:, t].rearrange("p g e -> p e g"), AX.X, ALU.add))
            st.sync()
            for t in range(3):
                st(ve.max(v8[:, t, :], lsel[:, t, :]))
            st.sync()
            for t in range(3):
                st(ve.max_index(ix8[:, t, :], v8[:, t, :], lsel[:, t, :]))
            ve.tensor_tensor(x1, v8[:, :, 1:2], v8[:, :, 0:1], ALU.subtract).then_inc(ex_in, 1)
            st.sync()
            st(ve.tensor_copy(eid, ix8[:, :, 0:2]))
            st(ve.tensor_scalar(gidx, gidx, float(EPG), None, ALU.mult))
            st.sync()
            st(ve.tensor_tensor(eid, eid, bc(gidx, 2, 2), ALU.add))
            st.sync()
            for k in range(2):
                st(ve.tensor_tensor(M[:, :, k, :], bc(iota32.unsqueeze(1), 1, 3), bc(eid[:, :, k:k + 1], 2, NE), ALU.is_equal))
            st.sync()
            st(ve.memset(M[NS:, 2], 0.0))
            st.sync()
            ve.tensor_tensor(M01, M[:, :, 0, :], M[:, :, 1, :], ALU.add).then_inc(m_ready, 1)
            dve.wait_ge(ex_out, 2)
            st(ve.tensor_reduce(u1[0], x4, AX.X, ALU.add))
            st(ve.tensor_scalar(u1[1], x1, 1.0, None, ALU.add))
            st.sync()
            st(ve.tensor_tensor(u1[2], u1[0], u1[1], ALU.mult))
            st.sync()
            st(ve.reciprocal(ewt[:, :, 0:1], u1[2]))
            st.sync()
            st(ve.tensor_tensor(ewt[:, :, 1:2], ewt[:, :, 0:1], x1, ALU.mult))
            dve.wait_ge(rank_done, 1)
            st(ve.tensor_copy(cnt, ps[:, 4, 3 * NE:4 * NE]))
            st.sync()
            st(ve.tensor_scalar(ov, cnt, CAP + 0.5, None, ALU.is_ge))
            for m in range(2, TO // CAP):
                st(ve.tensor_scalar(t32[(m - 2) % 2], cnt, CAP * m + 0.5, None, ALU.is_ge))
                st.sync()
                st(ve.tensor_tensor(ov, ov, t32[(m - 2) % 2], ALU.add))
            st.sync()
            st(ve.tensor_tensor_scan(ovc, ones[:, 0:NE], ov, 0.0, ALU.mult, ALU.add))
            for t in range(3):
                st(ve.tensor_tensor(Mx[:, t], M[:, t], bc(ps[:, 4, NE * t:NE * t + NE].unsqueeze(1), 1, 2), ALU.mult))
            st.sync()
            st(ve.tensor_tensor(ov, ovc, ov, ALU.subtract))
            st(ve.tensor_reduce(u2[0], Mx, AX.X, ALU.add))
            st.sync()
            for t in range(3):
                st(ve.tensor_tensor(Mx[:, t], M[:, t], bc(ov.unsqueeze(1), 1, 2), ALU.mult))
            st(ve.tensor_scalar(u2[2], u2[0], CAP - 0.5, None, ALU.is_ge))
            st.sync()
            st(ve.tensor_reduce(u2[1], Mx, AX.X, ALU.add))
            st(ve.scalar_tensor_tensor(out=u2[3], in0=eid, scalar=float(CAP), in1=u2[0], op0=ALU.mult, op1=ALU.add))
            st.sync()
            st(ve.tensor_tensor(u2[1], u2[1], eid, ALU.subtract))
            st.sync()
            st(ve.tensor_scalar(u2[1], u2[1], float(NE - 1), float(CAP), ALU.add, ALU.mult))
            st.sync()
            st(ve.tensor_tensor(u2[1], u2[1], u2[2], ALU.mult))
            st.sync()
            st(ve.tensor_tensor(u2[3], u2[3], u2[1], ALU.add))
            st.sync()
            ve.tensor_copy(destf, u2[3]).then_inc(dest_ready, 1)
            st.sync()
            st(ve.tensor_tensor(ovcmp[0:1], bc(ovc[0:1, :].unsqueeze(1), 1, 2 * NOP),
                                bc(iota32[0:1, 0:2 * NOP].unsqueeze(2), 2, NE), ALU.is_le))
            st(ve.tensor_scalar(novb[0:1], ovc[0:1, NE - 1:NE].broadcast_to([1, NE]), 0.5, None, ALU.mult))
            st.sync()
            st(ve.tensor_reduce(ovf[0:1], ovcmp[0:1], AX.X, ALU.add))
            st(ve.tensor_tensor(novb[0:1], novb[0:1], iota32[0:1], ALU.is_gt))
            st.sync()
            st(ve.tensor_scalar(ovf[0:1], ovf[0:1], float(NE - 1), None, ALU.min))
            st(ve.tensor_reduce(ov[0:1, 0:1], novb[0:1], AX.X, ALU.add))
            st.sync()
            st(ve.tensor_copy(ovexp[0:1], ovf[0:1]))
            st(ve.tensor_copy(novf[0:1], ov[0:1, 0:1]))
            st.sync()
            dve.sem_inc(small_done, 1)

            def to_diagonals():
                for t in range(3):
                    for k in range(4):
                        src = (destf, ewt)[k // 2][0:TR[t], t, k % 2:k % 2 + 1]
                        ve.tensor_scalar(diag[0:TR[t], t, k, 0:TR[t]], ident[0:TR[t], 0:TR[t]], src, None, ALU.mult)\
                            .then_inc(diag_ready, 1)

            def spread_copies():
                for i, dst in enumerate((slotB, ewtB)):
                    dve.wait_ge(spread_done, i + 1)
                    ve.tensor_copy(dst, ps[:, 4 + 2 * i:6 + 2 * i, 0:TO]).then_inc(spread_copied, 1)

            def way_back(m):
                if isinstance(m, int) and m == 0:
                    dve.wait_ge(spread_copied, 2)
                else:
                    dve.wait_ge(whalf, m)
                    ve.tensor_scalar(slotp, slotp, 2.0 * CAP, None, ALU.add).then_inc(wstep, 1)
                    dve.wait_ge(wstep, m)
                    dve.wait_ge(wsel_ready, m)
                    dve.wait_ge(sc_done, 6 * m)
                ve.scalar_tensor_tensor(out=Wh, in0=slotB, scalar=slotp, in1=ewtB, op0=ALU.is_equal, op1=ALU.mult)\
                    .then_inc(whalf, 1)
                dve.wait_ge(whalf, m + 1)
                ve.tensor_tensor(Wsel, Wh[:, 0], Wh[:, 1], ALU.add).then_inc(wsel_ready, 1)

            def add_part(m, i, last=False):
                t, j = i // 2, i % 2
                b_ = 0 if last and j else 4
                dve.wait_ge(sc_done, 6 * m + i + 1)
                d_ = hrow[0:TR[t], t, 1024 * j:1024 * j + 1024]
                ve.tensor_tensor(d_, d_, ps[0:TR[t], b_:b_ + 2, :].rearrange("p b c -> p (b c)"), ALU.add)\
                    .then_inc(last_added if last else sc_added, 1)

            def expert(m, half, inputs):
                n, first = 2 * m + half, isinstance(m, int) and m == 0
                back = half == 0 and not first
                if half == 0 and inputs is not None:
                    x_parts(inputs)
                    select(inputs + 1)
                    if first:
                        to_diagonals()
                if back:
                    for i in range(5):
                        add_part(m - 1, i)
                dve.wait_ge(weights_used, 12 * n + 8)
                ve.tensor_copy(GUs, ps[:, 0, :]).then_inc(gu_copied, 1)
                if half and inputs is not None:
                    x_parts(inputs)
                dve.wait_ge(silu_ready, n + 1)
                gt = ps[:, 1, :].rearrange("p (k x t) -> p k x t", k=4, x=2)
                ve.tensor_tensor(HT, Hs, gt[:, :, 1, :], ALU.mult).then_inc(hid_ready, 1)
                if back:
                    add_part(m - 1, 5)
                if first and not half:
                    spread_copies()
                if half == 0:
                    way_back(m)
                elif inputs is not None:
                    select(inputs + 1)
                dve.wait_ge(weights_used, 12 * (n + 1))
                if not first:
                    dve.wait_ge(sc_done, 6 * m)
                for x in range(2):
                    ve.tensor_copy(Os[CAP * half:CAP * half + CAP, 1024 + 512 * x:1536 + 512 * x],
                                   ps[CAP * x:CAP * x + CAP, 7, :]).then_inc(out_b, 1)

            def x_parts(m):
                for i in (1, 3):
                    dve.wait_ge(x_turned, 4 * m + i + 1)
                    ve.tensor_copy(xT[:, 4 * i:4 * i + 4].rearrange("p k t -> p (k t)"), ps[:, 3, :]).then_inc(xT_b, 1)

            def select(m):
                if not (isinstance(m, int) and m == 0):
                    dve.wait_ge(p_ready, 3 * m)
                    ve.tensor_scalar(slot, slot, 2.0 * CAP, None, ALU.add).then_inc(p_step, 1)
                    dve.wait_ge(p_step, m)
                for t in range(3):
                    ve.tensor_scalar(Psel[:, t], slot, destf[:, t, 0:1], None, ALU.is_equal).then_inc(p_half, 1)
                dve.wait_ge(p_half, 3 * m + 3)
                for t in range(3):
                    ve.scalar_tensor_tensor(out=Psel[:, t], in0=slot, scalar=destf[:, t, 1:2], in1=Psel[:, t],
                                            op0=ALU.is_equal, op1=ALU.add).then_inc(p_ready, 1)

            dve.wait_ge(dest_ready, 1)
            select(0)
            expert(0, 0, 0)
            expert(0, 1, 1)
            with dve.Fori(1, NPAIR - 1) as m:
                expert(m, 0, None)
                expert(m, 1, m + 1)
            expert(NPAIR - 1, 0, None)
            expert(NPAIR - 1, 1, None)
            n_over = dve.value_load(novf[0:1, 0:1], min_val=0, max_val=NOP)
            with dve.Fori(0, NOP) as o:
                with dve.If(n_over > o):
                    expert(o + NPAIR, 0, o + NPAIR)
                    expert(o + NPAIR, 1, None)
                dve.nop()
            dve.wait_ge(gfin_loaded, 16)

            def last_norm(t):
                rr = slice(0, TR[t])
                x_ = ssum[rr, 8 + t:9 + t]
                dve.wait_ge(fin_rstd[t], 1)
                ve.tensor_scalar(x_, x_, 1.0 / D, EPS, ALU.mult, ALU.add).then_inc(fin_ss[t], 1)
                dve.wait_ge(fin_rstd[t], 2)
                ve.reciprocal(ssum[rr, 12 + t:13 + t], x_).then_inc(fin_ss[t], 1)
                dve.wait_ge(fin_ss[t], 2)
                ve.scalar_tensor_tensor(out=hn[rr, t, :], in0=hrow[rr, t, :], scalar=ssum[rr, 12 + t:13 + t],
                                        in1=gfin[rr], op0=ALU.mult, op1=ALU.mult).then_inc(fin_ready, 1)

            for i in range(6):
                add_part(n_over + (NPAIR - 1), i, True)
                if i == 3:
                    last_norm(0)
            last_norm(1)
            last_norm(2)

        @block.tensor
        def _(pe):
            te = nc.tensor
            pe.wait_ge(ident_made, 1)
            pe.wait_ge(lam_loaded, 32)
            for r_ in range(2):
                mm = te.transpose(ps[:, 4, NJ * r_:NJ * r_ + NJ], lam_ld[:, r_, :], ident[0:NJ, 0:NJ])
            mm.then_inc(prm_turned, 1)
            for n in range(12):
                t, g = n // 4, n % 4
                pe.wait_ge(xn_scaled[t], 1)
                if n >= 4:
                    pe.wait_ge(xn_ready, n - 3)
                for k in range(4):
                    mm = te.transpose(ps[:, XB[n % 4], XT_ROWS * k:XT_ROWS * k + XT_ROWS],
                                      xr[:, t, 4 * g + k:D:KT], ident[0:XT_ROWS, 0:XT_ROWS])
                mm.then_inc(xn_turned, 1)
                if n == 11:
                    pe.wait_ge(s5_loaded, 16 * 6)
                    for m in range(4):
                        mm = te.transpose(ps[:, 7, 128 * m:128 * m + 128], st_ld[:, m, :], ident)
                    mm.then_inc(prm_turned, 1)
            pe.wait_ge(xn_ready, 12)

            def turn_pad(k):
                pe.wait_ge(pad_ready, k + 1)
                if k == 1:
                    pe.wait_ge(bt_ready, 4)
                for i in range(4):
                    if k == 1 and i >= 2:
                        pe.wait_ge(ct_ready, i - 1)
                    for x in range(4):
                        mm = te.transpose(ps[:, TB[k][i], 128 * x:128 * x + 128], pad[:, i // 2, 4 * (i % 2) + x, :], ident)
                    mm.then_inc(pad_turned, 1)

            def s5_in(j):
                c, q = j // 4, j % 4
                rows = slice(32 * q, 32 * q + 32)
                pe.wait_ge(proj_read, c + 1)
                if j == 0:
                    pe.wait_ge(bt_ready, 4)
                if j >= 2:
                    pe.wait_ge(bu_read, j - 1)
                for r_ in range(2):
                    te.matmul(ps[:, BU[j % 2][r_], 0:T], BT[rows, r_, c, :], uT[rows, c, :], start=True, stop=True)\
                      .then_inc(bu_done, 1)

            def s5_out(j):
                c, q = j // 4, j % 4
                cols_ = slice(32 * q, 32 * q + 32)
                pe.wait_ge(rotated, 2 * (j + 1))
                if j == 0:
                    pe.wait_ge(ct_ready, 4)
                if q == 0 and c >= 2:
                    pe.wait_ge(y_read, c - 1)
                for r_ in range(2):
                    mm = te.matmul(ps[cols_, YB[c % 2], 0:TO], CT[:, r_, c, cols_], Q1[j % 2][:, r_, N_META:T],
                                   start=(r_ == 0), stop=(r_ == 1))
                mm.then_inc(h_used, 1)

            def gla_front(c):
                f = FB[c % 2]
                if c == 0:
                    pe.wait_ge(gates_ready, 3)
                    pe.wait_ge(y_read, 8)
                    pe.wait_ge(masks_made, 2)
                if c >= 1:
                    pe.wait_ge(v_copied, c)
                if c >= 2:
                    pe.wait_ge(front_ready, 2 * (c - 1))
                for hf in range(2):
                    te.transpose(ps[:, 4, 128 * hf:128 * hf + 128], vT[:, hf, c, :], ident)
                te.transpose(ps[:, f, 256:384], chunk_view(kT[:, c]), ident)
                te.matmul(ps[:, f, 384:512], chunk_view(en[:, c]), chunk_view(qT[:, c]), start=True, stop=True)\
                  .then_inc(front_done, 1)

            def gla_back(c):
                sample = c >= NCP
                pe.wait_ge(v_copied, c + 1)
                pe.wait_ge(front_ready, 2 * (c + 1))
                if c >= 2:
                    pe.wait_ge(o_read, c - 1)
                if c >= 1:
                    pe.wait_ge(st_added, 2 * st_count(c))
                if sample:
                    pe.wait_ge(ss_loaded[c - NCP], 16 * SPC)
                if c:
                    te.matmul(ps[:, 6, 0:DV], PTm[c % 2], Vn[c % 2], start=True, stop=False, skip_group_check=True)
                    for s_ in range(SPC if sample else 1):
                        for h_ in range(H):
                            rows = slice(CL * h_, CL * h_ + CL)
                            lhs = qexp[:, h_, s_, :] if sample else qT[:, c, h_, :]
                            rhs = sstate[c - NCP][:, s_, h_] if sample else S[:, h_]
                            last = s_ == (SPC if sample else 1) - 1
                            mm = te.matmul(ps[rows, 6, 0:DV], lhs, rhs, start=False, stop=last, skip_group_check=True)
                    mm.then_inc(o_done, 1)
                n = 2 * SPC if sample else 2
                for i in range(n):
                    if i >= 2:
                        pe.wait_ge(st_added, 2 * (st_count(c) + i - 1))
                    for x in range(2):
                        if sample:
                            m = (2 * (i % 2) + x) * SPC + i // 2
                        else:
                            m = 2 * i + x
                        mm = te.matmul(ps[:, 2 + i % 2, 256 * x:256 * x + 256], Kexp[:, m, :], Vn[c % 2],
                                       start=True, stop=True)
                    mm.then_inc(st_done, 1)

            slot = 0
            for p, (kind, i) in enumerate(TILES):
                if p == PAD_B_TILE:
                    turn_pad(0)
                if p == PAD_C_TILE:
                    turn_pad(1)
                c = p - GLA_TILE0
                if 0 <= c < NCH:
                    gla_front(c)
                if p >= 2:
                    pe.wait_ge(proj_read, p - 1)
                n = CIDX[(kind, i // 2)] if kind in ("u", "q", "k", "v", "r", "glu") else None
                if n is not None and i % 2 == 0:
                    pe.wait_ge(ring_loaded[n % 2], 16 * (n // 2 + 1))
                if kind == "glu" and i == 0:
                    pe.wait_ge(z_ready, 1)
                if kind in ("a", "gk"):
                    pe.wait_ge(small_loaded, 6 * 16)
                kt = 8 if kind == "glu" else 1 if kind == "gk" else KT
                if kind == "gk":
                    pe.wait_ge(proj_read, TIDX[("a", 0)] + 1)
                for k in range(kt):
                    if k == (kt // 2 if kt > 1 else 0):
                        for j in bu_at[2 * p + 1]:
                            s5_in(j)
                        for j in y_at[2 * p + 1]:
                            s5_out(j)
                        if 0 <= c < NCH:
                            gla_back(c)
                    if k == 0:
                        for j in bu_at[2 * p]:
                            s5_in(j)
                        for j in y_at[2 * p]:
                            s5_out(j)
                    out = ps[:, p % 2, 0:T]
                    if kind == "a":
                        mm = te.matmul(ps[0:RANK, p % 2, 0:T], wa[:, k, :], xnT[:, k, :], start=(k == 0), stop=(k == kt - 1))
                    elif kind == "gk":
                        mm = te.matmul(out, wgk[:, DK * i:DK * i + DK], aT, start=True, stop=True)
                    else:
                        w = ring[n % 2][:, 0:256 * kt].rearrange("p (k n) -> p k n", n=256)[:, k, 128 * (i % 2):128 * (i % 2) + 128]
                        x = zT[:, k, :] if kind == "glu" else xnT[:, k, N_META:T] if kind == "r" else xnT[:, k, :]
                        o = out if kind not in ("r", "glu") else out[:, 0:TO]
                        mm = te.matmul(o, w, x, start=(k == 0), stop=(k == kt - 1))
                mm.then_inc(proj_done, 1)
            pe.wait_ge(hl_saved, NJ)
            pe.wait_ge(st_added, 2 * st_count(NCH))
            for r_ in range(2):
                te.transpose(ps[0:NJ, 2 + r_, 0:128], hl[:, r_, 0, :], ident)
                for m in range(2):
                    mm = te.transpose(ps[:, 2 + r_, 128 + 128 * m:256 + 128 * m],
                                      hl[:, r_, 1 + 4 * m:5 + 4 * m, :].rearrange("p s j -> p (s j)"), ident)
                mm.then_inc(hl_turned, 1)
            pe.wait_ge(hl_copied, 2)
            for c in range(NCH - 1):
                pe.wait_ge(o_scaled, c + 1)
                for hf in range(2):
                    n = 2 * c + hf
                    if n >= 4:
                        pe.wait_ge(mix_gla, n - 3)
                    te.transpose(ps[:, XB[n % 4], 0:128], o_all[:, c, 128 * hf:128 * hf + 128], ident).then_inc(o_turned, 1)
            pe.wait_ge(mix_s5, 8)
            pe.wait_ge(mix_gla, 2 * (NCH - 1))
            for i in range(8):
                n = CIDX[("out", i)]
                pe.wait_ge(ring_loaded[n % 2], 16 * (n // 2 + 1))
                w = ring[n % 2].rearrange("p (k n) -> p k n", n=256)
                for t in range(3):
                    if i >= 2:
                        pe.wait_ge(h_added, 3 * (i - 2) + t + 1)
                    for m in range(16):
                        if t < 2:
                            mm = te.matmul(ps[:, OB[i % 2][t], 0:256], mixT[:, m, 128 * t:128 * t + 128], w[:, m, :],
                                           start=(m == 0), stop=(m == 15))
                        else:
                            for x in range(2):
                                mm = te.matmul(ps[NS * x:NS * x + NS, OB[i % 2][t], 0:128], mixT[:, m, SEQ:TO],
                                               w[:, m, 128 * x:128 * x + 128], start=(m == 0), stop=(m == 15))
                    mm.then_inc(wout_done, 1)
            pe.wait_ge(h_added, 24)
            for n in range(12):
                t, g_ = n // 4, n % 4
                pe.wait_ge(hn_ready, t + 1)
                if n >= 4:
                    pe.wait_ge(hnT_ready, n - 3)
                for k in range(4):
                    mm = te.transpose(ps[:, XB[n % 4], TR[t] * k:TR[t] * k + TR[t]], hn[0:TR[t], t, 4 * g_ + k:D:KT],
                                      ident[0:TR[t], 0:TR[t]])
                mm.then_inc(hn_turned, 1)
            pe.wait_ge(hnT_ready, 12)
            for k in range(KT):
                mm = te.matmul(ps[64 * (k % 2):64 * (k % 2) + NL, 7, 0:TO], Wr[:, k, :], hnT[:, k, :],
                               start=(k < 2), stop=(k >= KT - 2))
            mm.then_inc(logits_done, 1)
            pe.wait_ge(logitsT_ready, 2)
            for t in range(3):
                mm = te.transpose(ps[0:TR[t], 4, NL * t:NL * t + NL], logT[:, 0, 128 * t:128 * t + TR[t]], ident[0:NL, 0:NL])
            mm.then_inc(logits_turned, 1)
            pe.wait_ge(m_ready, 1)
            for t in range(4):
                for t2 in range(min(t + 1, 3)):
                    mm = te.matmul(ps[:, 4, NE * t:NE * t + NE], tri16 if t2 == t else ones16, M01[:, t2, :],
                                   start=(t2 == 0), stop=(t2 == min(t, 2)))
            mm.then_inc(rank_done, 1)

            def gather(m, quarters=range(4)):
                pe.wait_ge(p_ready, 3 * (m + 1))
                for i in quarters:
                    if i == 2:
                        pe.wait_ge(xT_a, 2 * m + 1)
                    if i == 3:
                        pe.wait_ge(xT_b, 2 * m + 1)
                    for k in range(4):
                        for t in range(3):
                            mm = te.matmul(ps[:, 2 + i % 2, 2 * CAP * k:2 * CAP * (k + 1)], hn[:, t, 4 * i + k:D:KT],
                                           Psel[:, t, :], start=(t == 0), stop=(t == 2))
                    mm.then_inc(x_turned, 1)

            def spread():
                pe.wait_ge(diag_ready, 12)
                for k in range(4):
                    for t in range(3):
                        mm = te.matmul(ps[:, 4 + k, 128 * t:128 * t + TR[t]], ones[0:TR[t], :],
                                       diag[0:TR[t], t, k, 0:TR[t]], start=True, stop=True)
                    if k % 2:
                        mm.then_inc(spread_done, 1)

            def add_back(m, i, last=False):
                t, j = i // 2, i % 2
                b_ = 0 if last and i % 2 else 4
                if i == 0:
                    pe.wait_ge(out_a, 4 * m + 4)
                    pe.wait_ge(out_b, 4 * m + 4)
                    pe.wait_ge(wsel_ready, m + 1)
                elif not last:
                    pe.wait_ge(sc_added, 6 * m + i)
                elif i >= 2:
                    pe.wait_ge(last_added, i - 1)
                for x in range(2):
                    mm = te.matmul(ps[0:TR[t], b_ + x, :], Wsel[:, 128 * t:128 * t + TR[t]],
                                   Os[:, 1024 * j + 512 * x:1024 * j + 512 * x + 512], start=True, stop=True)
                mm.then_inc(sc_done, 1)

            def expert(m, half, inputs):
                n, first = 2 * m + half, isinstance(m, int) and m == 0
                back = half == 0 and not first
                start = first and not half
                if start:
                    gather(0, range(2))
                else:
                    if half == 0 and inputs is not None:
                        gather(inputs)
                    pe.wait_ge(xT_a, 2 * m + 2)
                    pe.wait_ge(xT_b, 2 * m + 2)
                for q in range(4):
                    if start:
                        pe.wait_ge((xT_a, xT_b)[q % 2], q // 2 + 1)
                    pe.wait_ge(piece_loaded[2 * q], 16 * (n + 1))
                    pe.wait_ge(piece_loaded[2 * q + 1], 16 * (n + 1))
                    for k in range(4):
                        for x in range(2):
                            mm = te.matmul(ps[CAP * x:CAP * x + CAP, 0, :],
                                           xT[:, 4 * q + k, CAP * half:CAP * half + CAP],
                                           wpiece[2 * q + x][:, HID * k:HID * k + HID],
                                           start=(q == 0 and k == 0), stop=(q == 3 and k == 3))
                        if k == 3:
                            mm.then_inc(weights_used, 2)
                        if back and k % 2 and q in (1, 2):
                            add_back(m - 1, 2 * (q - 1) + k // 2)
                    if start and q < 2:
                        gather(0, range(2 + q, 3 + q))
                if start:
                    spread()
                elif back:
                    add_back(m - 1, 4)
                elif inputs is not None:
                    gather(inputs)
                pe.wait_ge(gu_copied, n + 1)
                for k in range(4):
                    mm = te.transpose(ps[:, 1, 128 * k:128 * k + 128], GUs[:, k:HID:4], ident)
                mm.then_inc(gu_turned, 1)
                if back:
                    add_back(m - 1, 5)
                pe.wait_ge(hid_ready, n + 1)
                if start:
                    pe.wait_ge(spread_copied, 2)
                else:
                    pe.wait_ge(out_a, 2 * n)
                    pe.wait_ge(out_b, 2 * n)
                for k in range(4):
                    pe.wait_ge(piece_loaded[8 + k], 16 * (n + 1))
                    for j in range(2):
                        for x in range(2):
                            mm = te.matmul(ps[CAP * x:CAP * x + CAP, 6 + j, :], HT[:, k, :],
                                           wpiece[8 + k][:, 512 * (2 * j + x):512 * (2 * j + x) + 512],
                                           start=(k == 0), stop=(k == 3))
                    mm.then_inc(weights_used, 1)

            expert(0, 0, 0)
            expert(0, 1, 1)
            with pe.Fori(1, NPAIR - 1) as m:
                expert(m, 0, None)
                expert(m, 1, m + 1)
            expert(NPAIR - 1, 0, None)
            expert(NPAIR - 1, 1, None)
            pe.wait_ge(small_done, 1)
            n_over = pe.value_load(novf[0:1, 0:1], min_val=0, max_val=NOP)
            with pe.Fori(0, NOP) as o:
                with pe.If(n_over > o):
                    expert(o + NPAIR, 0, o + NPAIR)
                    expert(o + NPAIR, 1, None)
                pe.nop()
            for i in range(6):
                add_back(n_over + (NPAIR - 1), i, True)


_INS = ["x_prompt", "x_sample", "state_gla", "state_s5_re", "state_s5_im", "meta", "g_mix", "w_in", "w_gk2", "b_gk",
        "g_gla", "lam_re", "lam_im", "log_dt", "s5_b_re", "s5_b_im", "s5_c_re", "s5_c_im", "d_skip", "w_glu", "b_glu",
        "w_out", "g_ffn", "w_rg", "b_rg", "w_re", "b_re", "w_gate", "w_up", "w_down", "g_final"]
_OUTS = {"y_prompt": (1, 256, 2048), "y_sample": (8, 8, 2048), "new_gla_prompt": (1, 1, 4, 128, 256),
         "new_s5_re_prompt": (1, 1, 64, 64), "new_s5_im_prompt": (1, 1, 64, 64), "new_gla_sample": (1, 8, 4, 128, 256),
         "new_s5_re_sample": (1, 8, 64, 64), "new_s5_im_sample": (1, 8, 64, 64)}


def kernel(**inputs):
    import numpy as _np
    import concourse.bacc as _bacc
    from concourse import mybir as _mybir
    from concourse.bass_utils import run_bass_kernel_spmd as _run

    nc = _bacc.Bacc("TRN2", target_bir_lowering=False, num_devices=1)
    arrays, args = {}, {}
    for name in _INS:
        a = _np.ascontiguousarray(inputs[name])
        arrays[f"in_{name}"] = a
        args[name] = nc.dram_tensor(f"in_{name}", a.shape, _mybir.dt.from_np(a.dtype), kind="ExternalInput").ap()
    for name, shape in _OUTS.items():
        args[name] = nc.dram_tensor(f"out_{name}", shape, _mybir.dt.float32, kind="ExternalOutput").ap()
    build(nc, args)
    r = _run(nc, [arrays], core_ids=[0])
    return tuple(r.results[0][f"out_{name}"] for name in _OUTS)
```
